# Optimizing a Trainium2 kernel written in Bass

```python
import jax, jax.numpy as jnp
from jax import lax
import numpy as np

D_MODEL = 1024
BATCH = 1
SEQ = 256
DEPTH = 2

N_MIXERS = 2
EPS = 1e-6
LRU_WIDTH = 1280
LRU_BLOCKS = 10
LRU_BLOCK_W = LRU_WIDTH // LRU_BLOCKS
LRU_CONV = 4
LRU_C = 8.0
N_HEADS = 16
HEAD_DIM = 64
N_KV = 4
GROUP = N_HEADS // N_KV
N_BRANCH = 3
CMP_BLOCK = 32
CMP_STRIDE = 16
CMP_HIDDEN = 256
SEL_BLOCK = 64
N_SELECT = 8
WINDOW = 512
Q_BLOCK = 64
FORCED_BONUS = 1e4
NEG = -1e30
Q_COLS = N_HEADS * HEAD_DIM
KV_COLS = 2 * N_KV * HEAD_DIM
NSA_IN = Q_COLS + N_BRANCH * KV_COLS + N_BRANCH * N_HEADS
D_FF = 3072
FFN_CONV = 3


def rmsnorm(x, g):
    xf = x.astype(jnp.float32)
    y = xf * lax.rsqrt(jnp.mean(xf * xf, axis=-1, keepdims=True) + EPS)
    return (y * g.astype(jnp.float32)).astype(x.dtype)

def causal_dwconv(x, w, b):
    K, C = w.shape
    y = lax.conv_general_dilated(x, w[:, None, :].astype(x.dtype), window_strides=(1,),
                                 padding=[(K - 1, 0)], dimension_numbers=('NWC', 'WIO', 'NWC'),
                                 feature_group_count=C)
    return y + b.astype(x.dtype)

def alibi_slopes():
    s = 2.0 ** (-8.0 * np.arange(1, N_HEADS + 1) / N_HEADS)
    return jnp.asarray(s, dtype=jnp.float32).reshape(N_KV, GROUP)

def masked_softmax(s, m):
    return jax.nn.softmax(jnp.where(m, s, NEG), axis=-1)

def rglru_mixer(x, w_in, conv_w, conv_b, gate_w, gate_b, a_param, w_out):
    B, S, _ = x.shape
    y_br, x_br = jnp.split(x @ w_in, 2, axis=-1)
    y_br = jax.nn.gelu(y_br)
    xc = causal_dwconv(x_br, conv_w, conv_b)
    xb = xc.reshape(B, S, LRU_BLOCKS, LRU_BLOCK_W)
    g = jnp.einsum('bsnc,gncd->gbsnd', xb, gate_w).reshape(2, B, S, LRU_WIDTH)
    g = jax.nn.sigmoid(g.astype(jnp.float32) + gate_b.astype(jnp.float32)[:, None, None, :])
    r_gate, i_gate = g[0], g[1]
    log_a = -LRU_C * r_gate * jax.nn.softplus(-a_param.astype(jnp.float32))
    a = jnp.exp(log_a)
    mult = jnp.sqrt(-jnp.expm1(2.0 * log_a))
    bterm = mult * i_gate * xc.astype(jnp.float32)

    def combine(left, right):
        a1, b1 = left
        a2, b2 = right
        return a1 * a2, a2 * b1 + b2

    _, h = lax.associative_scan(combine, (a, bterm), axis=1)
    return (h.astype(x.dtype) * y_br) @ w_out

def nsa_mixer(x, w_in, cmp_pos, cmp_w1, cmp_b1, cmp_w2, w_out):
    B, S, _ = x.shape
    dt = x.dtype
    f32 = jnp.float32
    proj = x @ w_in
    q = proj[..., :Q_COLS].reshape(B, S, N_KV, GROUP, HEAD_DIM).transpose(0, 2, 3, 1, 4)
    q = q * (HEAD_DIM ** -0.5)
    kv = proj[..., Q_COLS:Q_COLS + N_BRANCH * KV_COLS].reshape(B, S, N_BRANCH, 2, N_KV, HEAD_DIM)
    kv = kv.transpose(2, 3, 0, 4, 1, 5)
    gates = jax.nn.sigmoid(proj[..., Q_COLS + N_BRANCH * KV_COLS:].astype(f32))
    gates = gates.reshape(B, S, N_BRANCH, N_KV, GROUP).transpose(2, 0, 3, 4, 1)
    slopes = alibi_slopes()

    n_cmp = (S - CMP_BLOCK) // CMP_STRIDE + 1
    cmp_start = jnp.arange(n_cmp) * CMP_STRIDE
    tok_idx = cmp_start[:, None] + jnp.arange(CMP_BLOCK)[None, :]

    def compress(t, pos, w1, b1, w2):
        blk = (t[:, :, tok_idx] + pos.astype(dt)).reshape(B, N_KV, n_cmp, CMP_BLOCK * HEAD_DIM)
        return jax.nn.gelu(blk @ w1 + b1.astype(dt)) @ w2

    k_cmp = compress(kv[0, 0], cmp_pos[0], cmp_w1[0], cmp_b1[0], cmp_w2[0])
    v_cmp = compress(kv[0, 1], cmp_pos[1], cmp_w1[1], cmp_b1[1], cmp_w2[1])
    cmp_end = cmp_start + CMP_BLOCK - 1
    cmp_center = cmp_start.astype(f32) + (CMP_BLOCK - 1) / 2.0

    n_sel = S // SEL_BLOCK
    n_top = min(N_SELECT, n_sel)
    sel_j = jnp.arange(n_sel)
    overlap = ((cmp_start[:, None] < (sel_j[None, :] + 1) * SEL_BLOCK) &
               (cmp_start[:, None] + CMP_BLOCK > sel_j[None, :] * SEL_BLOCK)).astype(f32)
    k_blocks = kv[1, 0].reshape(B, N_KV, n_sel, SEL_BLOCK, HEAD_DIM)
    v_blocks = kv[1, 1].reshape(B, N_KV, n_sel, SEL_BLOCK, HEAD_DIM)
    gather = jax.vmap(jax.vmap(lambda blk, ix: blk[ix]))

    pad = ((0, 0), (0, 0), (WINDOW, 0), (0, 0))
    k_win = jnp.pad(kv[2, 0], pad)
    v_win = jnp.pad(kv[2, 1], pad)

    def query_block(q0):
        qc = lax.dynamic_slice_in_dim(q, q0, Q_BLOCK, axis=3)
        gc = lax.dynamic_slice_in_dim(gates, q0, Q_BLOCK, axis=4)
        t = q0 + jnp.arange(Q_BLOCK)
        tf = t.astype(f32)
        sl = slopes[:, :, None, None]

        m_c = cmp_end[None, :] <= t[:, None]
        s = jnp.einsum('bgrqd,bgcd->bgrqc', qc, k_cmp, preferred_element_type=f32)
        s = s - sl * (tf[:, None] - cmp_center[None, :])
        p_cmp = masked_softmax(s, m_c) * m_c
        o_cmp = jnp.einsum('bgrqc,bgcd->bgrqd', p_cmp.astype(dt), v_cmp)

        imp = jnp.einsum('bgrqc,cj->bgqj', p_cmp, overlap)
        cur = t // SEL_BLOCK
        forced = (sel_j[None, :] == 0) | (sel_j[None, :] == cur[:, None]) | (sel_j[None, :] == cur[:, None] - 1)
        future = sel_j[None, :] > cur[:, None]
        score = jnp.where(forced, FORCED_BONUS, jnp.where(future, -1.0, imp))
        _, idx = lax.top_k(score, n_top)
        kg = gather(k_blocks, idx).reshape(B, N_KV, Q_BLOCK, n_top * SEL_BLOCK, HEAD_DIM)
        vg = gather(v_blocks, idx).reshape(B, N_KV, Q_BLOCK, n_top * SEL_BLOCK, HEAD_DIM)
        pos = (idx[..., None] * SEL_BLOCK + jnp.arange(SEL_BLOCK)).reshape(B, N_KV, Q_BLOCK, n_top * SEL_BLOCK)
        dist = (t[:, None] - pos)[:, :, None]
        s = jnp.einsum('bgrqd,bgqkd->bgrqk', qc, kg, preferred_element_type=f32)
        s = s - sl * dist.astype(f32)
        p = masked_softmax(s, dist >= 0)
        o_sel = jnp.einsum('bgrqk,bgqkd->bgrqd', p.astype(dt), vg)

        kw = lax.dynamic_slice_in_dim(k_win, q0, WINDOW + Q_BLOCK, axis=2)
        vw = lax.dynamic_slice_in_dim(v_win, q0, WINDOW + Q_BLOCK, axis=2)
        pos_w = q0 - WINDOW + jnp.arange(WINDOW + Q_BLOCK)
        dist_w = t[:, None] - pos_w[None, :]
        m_w = (dist_w >= 0) & (dist_w < WINDOW) & (pos_w[None, :] >= 0)
        s = jnp.einsum('bgrqd,bgkd->bgrqk', qc, kw, preferred_element_type=f32)
        s = s - sl * dist_w.astype(f32)
        p = masked_softmax(s, m_w)
        o_win = jnp.einsum('bgrqk,bgkd->bgrqd', p.astype(dt), vw)

        o = (gc[0][..., None] * o_cmp.astype(f32) + gc[1][..., None] * o_sel.astype(f32)
             + gc[2][..., None] * o_win.astype(f32)).astype(dt)
        return o.transpose(0, 3, 1, 2, 4).reshape(B, Q_BLOCK, Q_COLS)

    starts = jnp.arange(S // Q_BLOCK) * Q_BLOCK
    o = lax.map(query_block, starts)
    o = o.transpose(1, 0, 2, 3).reshape(B, S, Q_COLS)
    return o @ w_out

def conv_ffn(x, w_in, conv_w, conv_b, w_out):
    a, b = jnp.split(x @ w_in, 2, axis=-1)
    a = causal_dwconv(a, conv_w, conv_b)
    return (jax.nn.gelu(a) * b) @ w_out

def first_inputs(seed: int = 0) -> dict:
    key = jax.random.key(seed)
    ks = iter(jax.random.split(key, 32))
    n_a = len(range(0, DEPTH, N_MIXERS))
    n_b = len(range(1, DEPTH, N_MIXERS))

    def nrm(shape, scale):
        return jax.random.normal(next(ks), shape, jnp.float32) * scale

    def gain(shape):
        return 1.0 + nrm(shape, 0.05)

    x = nrm((BATCH, SEQ, D_MODEL), 1.0)
    lru_norm_g = gain((n_a, D_MODEL))
    lru_w_in = nrm((n_a, D_MODEL, 2 * LRU_WIDTH), D_MODEL ** -0.5)
    lru_conv_w = nrm((n_a, LRU_CONV, LRU_WIDTH), LRU_CONV ** -0.5)
    lru_conv_b = nrm((n_a, LRU_WIDTH), 0.02)
    lru_gate_w = nrm((n_a, 2, LRU_BLOCKS, LRU_BLOCK_W, LRU_BLOCK_W), LRU_BLOCK_W ** -0.5)
    lru_gate_b = nrm((n_a, 2, LRU_WIDTH), 0.1)
    a_c = jax.random.uniform(next(ks), (n_a, LRU_WIDTH), jnp.float32, 0.9, 0.999)
    s = a_c ** (1.0 / LRU_C)
    lru_a_param = jnp.log(s) - jnp.log1p(-s)
    lru_w_out = nrm((n_a, LRU_WIDTH, D_MODEL), LRU_WIDTH ** -0.5)
    nsa_norm_g = gain((n_b, D_MODEL))
    nsa_w_in = nrm((n_b, D_MODEL, NSA_IN), D_MODEL ** -0.5)
    nsa_cmp_pos = nrm((n_b, 2, CMP_BLOCK, HEAD_DIM), 0.1)
    nsa_cmp_w1 = nrm((n_b, 2, CMP_BLOCK * HEAD_DIM, CMP_HIDDEN), (CMP_BLOCK * HEAD_DIM) ** -0.5)
    nsa_cmp_b1 = nrm((n_b, 2, CMP_HIDDEN), 0.02)
    nsa_cmp_w2 = nrm((n_b, 2, CMP_HIDDEN, HEAD_DIM), CMP_HIDDEN ** -0.5)
    nsa_w_out = nrm((n_b, Q_COLS, D_MODEL), Q_COLS ** -0.5)
    ffn_norm_g = gain((DEPTH, D_MODEL))
    ffn_w_in = nrm((DEPTH, D_MODEL, 2 * D_FF), D_MODEL ** -0.5)
    ffn_conv_w = nrm((DEPTH, FFN_CONV, D_FF), FFN_CONV ** -0.5)
    ffn_conv_b = nrm((DEPTH, D_FF), 0.02)
    ffn_w_out = nrm((DEPTH, D_FF, D_MODEL), D_FF ** -0.5)
    final_norm_g = gain((D_MODEL,))
    return {"x": x, "lru_norm_g": lru_norm_g, "lru_w_in": lru_w_in, "lru_conv_w": lru_conv_w,
            "lru_conv_b": lru_conv_b, "lru_gate_w": lru_gate_w, "lru_gate_b": lru_gate_b,
            "lru_a_param": lru_a_param, "lru_w_out": lru_w_out, "nsa_norm_g": nsa_norm_g,
            "nsa_w_in": nsa_w_in, "nsa_cmp_pos": nsa_cmp_pos, "nsa_cmp_w1": nsa_cmp_w1,
            "nsa_cmp_b1": nsa_cmp_b1, "nsa_cmp_w2": nsa_cmp_w2, "nsa_w_out": nsa_w_out,
            "ffn_norm_g": ffn_norm_g, "ffn_w_in": ffn_w_in, "ffn_conv_w": ffn_conv_w,
            "ffn_conv_b": ffn_conv_b, "ffn_w_out": ffn_w_out, "final_norm_g": final_norm_g}

def first_block(x, lru_norm_g, lru_w_in, lru_conv_w, lru_conv_b, lru_gate_w, lru_gate_b,
              lru_a_param, lru_w_out, nsa_norm_g, nsa_w_in, nsa_cmp_pos, nsa_cmp_w1,
              nsa_cmp_b1, nsa_cmp_w2, nsa_w_out, ffn_norm_g, ffn_w_in, ffn_conv_w,
              ffn_conv_b, ffn_w_out, final_norm_g):
    h = x
    for layer in range(DEPTH):
        mixer, j = layer % N_MIXERS, layer // N_MIXERS
        if mixer == 0:
            h = h + rglru_mixer(rmsnorm(h, lru_norm_g[j]), lru_w_in[j], lru_conv_w[j], lru_conv_b[j],
                                lru_gate_w[j], lru_gate_b[j], lru_a_param[j], lru_w_out[j])
        else:
            h = h + nsa_mixer(rmsnorm(h, nsa_norm_g[j]), nsa_w_in[j], nsa_cmp_pos[j], nsa_cmp_w1[j],
                              nsa_cmp_b1[j], nsa_cmp_w2[j], nsa_w_out[j])
        h = h + conv_ffn(rmsnorm(h, ffn_norm_g[layer]), ffn_w_in[layer], ffn_conv_w[layer],
                         ffn_conv_b[layer], ffn_w_out[layer])
    return rmsnorm(h, final_norm_g)


GRID_W = 64
CTX_LEN = 256
CONV_W = 512
CONV_K = 31
NA_HEADS = 8
NA_W = NA_HEADS * HEAD_DIM
NA_KH_MAX = 8
NA_KW = 16
NA_QCW = 16
NA_KCW = 32
NA_NCB = GRID_W // NA_QCW
GQA_Q_HEADS = 8
GQA_KV_HEADS = 2
GQA_Q_W = GQA_Q_HEADS * HEAD_DIM
GQA_KV_W = GQA_KV_HEADS * HEAD_DIM
Q_BLOCK_2 = 128
FFN_HIDDEN = ((8 * D_MODEL + 767) // 768) * 256
ROPE_THETA = 10000.0
NEG_2 = -1e30
IN_SPLITS = (2 * CONV_W, NA_W, NA_W, NA_W, GQA_Q_W, GQA_KV_W, GQA_KV_W, N_BRANCH * D_MODEL)
IN_WIDTH = sum(IN_SPLITS)


def rmsnorm_2(x, g):
    xf = x.astype(jnp.float32)
    y = xf * lax.rsqrt(jnp.mean(xf * xf, axis=-1, keepdims=True) + EPS)
    return (y * g.astype(jnp.float32)).astype(x.dtype)

def layernorm(x, g, b):
    xf = x.astype(jnp.float32)
    mu = jnp.mean(xf, axis=-1, keepdims=True)
    var = jnp.mean(jnp.square(xf - mu), axis=-1, keepdims=True)
    y = (xf - mu) * lax.rsqrt(var + EPS)
    return (y * g.astype(jnp.float32) + b.astype(jnp.float32)).astype(x.dtype)

def modulate(h, shift, scale):
    return h * (1 + scale) + shift

def split_in(p):
    return jnp.split(p, np.cumsum(IN_SPLITS)[:-1].tolist(), axis=-1)

def heads(t, n):
    return t.reshape(t.shape[:-1] + (n, HEAD_DIM))

def axial_rope(x, pos_row, pos_col):
    half = x.shape[-1] // 2
    freqs = jnp.power(ROPE_THETA, -jnp.arange(0, half, 2, dtype=jnp.float32) / half)

    def rot(xa, pos):
        ang = pos[:, None] * freqs
        cos = jnp.cos(ang)[None, :, None, :].astype(x.dtype)
        sin = jnp.sin(ang)[None, :, None, :].astype(x.dtype)
        x1, x2 = jnp.split(xa, 2, axis=-1)
        return jnp.concatenate([x1 * cos - x2 * sin, x1 * sin + x2 * cos], axis=-1)

    return jnp.concatenate([rot(x[..., :half], pos_row), rot(x[..., half:], pos_col)], axis=-1)

def conv_branch(a, conv_w, conv_b, ln_g, ln_b, w_out):
    u = a[..., :CONV_W] * jax.nn.sigmoid(a[..., CONV_W:])
    y = lax.conv_general_dilated(
        u, conv_w[:, None, :], window_strides=(1,), padding=[(CONV_K // 2, CONV_K // 2)],
        dimension_numbers=("NWC", "WIO", "NWC"), feature_group_count=CONV_W) + conv_b
    y = jax.nn.silu(layernorm(y, ln_g, ln_b))
    return y @ w_out

def dense_attention(q, k, v):
    B, T, Hq, dh = q.shape
    Hkv = k.shape[2]
    qg = q.reshape(B, T, Hkv, Hq // Hkv, dh) * (dh ** -0.5)
    s = jnp.einsum("bqhgd,bkhd->bhgqk", qg, k).astype(jnp.float32)
    p = jax.nn.softmax(s, axis=-1).astype(v.dtype)
    return jnp.einsum("bhgqk,bkhd->bqhgd", p, v).reshape(B, T, Hq * dh)

def gqa_latent(q, k, v, kc, vc):
    B, S, Hq, dh = q.shape
    Hkv = k.shape[2]
    G = Hq // Hkv
    k_all = jnp.concatenate([k, kc], axis=1)
    v_all = jnp.concatenate([v, vc], axis=1)
    nblk = S // Q_BLOCK_2
    qb = jnp.moveaxis((q * (dh ** -0.5)).reshape(B, nblk, Q_BLOCK_2, Hkv, G, dh), 1, 0)

    def one_block(q_blk):
        s = jnp.einsum("bqhgd,bkhd->bhgqk", q_blk, k_all).astype(jnp.float32)
        p = jax.nn.softmax(s, axis=-1).astype(v.dtype)
        return jnp.einsum("bhgqk,bkhd->bqhgd", p, v_all)

    o = lax.map(one_block, qb)
    return jnp.moveaxis(o, 0, 1).reshape(B, S, Hq * dh)

def na_latent(q, k, v, kc, vc, rpb):
    B, S, H, dh = q.shape
    rows = S // GRID_W
    kh = min(NA_KH_MAX, rows)
    q_cols = np.arange(GRID_W).reshape(NA_NCB, NA_QCW)
    key_cols = (np.clip(np.arange(NA_NCB) * NA_QCW - NA_KW // 2, 0, GRID_W - NA_KCW)[:, None]
                + np.arange(NA_KCW))
    win0 = np.clip(q_cols - NA_KW // 2, 0, GRID_W - NA_KW)[..., None]
    kcols = key_cols[:, None, :]
    col_mask = jnp.asarray((kcols >= win0) & (kcols < win0 + NA_KW))
    col_bias_idx = np.clip(kcols - q_cols[..., None] + NA_KW - 1, 0, 2 * NA_KW - 2)
    qg = (q * (dh ** -0.5)).reshape(B, rows, NA_NCB, NA_QCW, H, dh)
    kg = k.reshape(B, rows, GRID_W, H, dh)
    vg = v.reshape(B, rows, GRID_W, H, dh)
    n_loc = kh * NA_KCW

    def one_row(r):
        r0 = jnp.clip(r - kh // 2, 0, rows - kh)
        kb = lax.dynamic_slice_in_dim(kg, r0, kh, axis=1)[:, :, key_cols]
        vb = lax.dynamic_slice_in_dim(vg, r0, kh, axis=1)[:, :, key_cols]
        qr = lax.dynamic_index_in_dim(qg, r, axis=1, keepdims=False)
        drow = r0 + jnp.arange(kh) - r + NA_KH_MAX - 1
        bias = rpb[:, drow][:, :, col_bias_idx].transpose(0, 2, 3, 1, 4)
        s_loc = jnp.einsum("bnqhd,bknchd->bhnqkc", qr, kb).astype(jnp.float32) + bias.astype(jnp.float32)
        s_loc = jnp.where(col_mask[:, :, None, :], s_loc, NEG_2).reshape(B, H, NA_NCB, NA_QCW, n_loc)
        s_ctx = jnp.einsum("bnqhd,bthd->bhnqt", qr, kc).astype(jnp.float32)
        p = jax.nn.softmax(jnp.concatenate([s_loc, s_ctx], axis=-1), axis=-1).astype(v.dtype)
        p_loc = p[..., :n_loc].reshape(B, H, NA_NCB, NA_QCW, kh, NA_KCW)
        p_ctx = p[..., n_loc:]
        return (jnp.einsum("bhnqkc,bknchd->bnqhd", p_loc, vb)
                + jnp.einsum("bhnqt,bthd->bnqhd", p_ctx, vc))

    o = lax.map(one_row, jnp.arange(rows))
    return jnp.moveaxis(o, 0, 1).reshape(B, S, H * dh)

def merge(br_a, br_b, br_c, gates, w_out):
    ga, gb, gc = jnp.split(gates, N_BRANCH, axis=-1)
    y = jax.nn.sigmoid(ga) * br_a + jax.nn.sigmoid(gb) * br_b + jax.nn.sigmoid(gc) * br_c
    return y @ w_out

def swiglu(h, w_in, w_out):
    gate, up = jnp.split(h @ w_in, 2, axis=-1)
    return (jax.nn.silu(gate) * up) @ w_out

def second_inputs(seed: int = 0) -> dict:
    key = jax.random.key(seed)
    ks = jax.random.split(key, 23)
    L, D = DEPTH, D_MODEL

    def nrm(k, shape, s):
        return jax.random.normal(k, shape, jnp.float32) * s

    return {
        "x": nrm(ks[0], (BATCH, SEQ, D), 1.0),
        "c": nrm(ks[1], (BATCH, D), 1.0),
        "ctx": nrm(ks[2], (BATCH, CTX_LEN, D), 1.0),
        "c_ctx": nrm(ks[3], (D,), 1.0),
        "w_mod": nrm(ks[4], (L, D, 6 * D), 0.5 * D ** -0.5),
        "b_mod": nrm(ks[5], (L, 6 * D), 0.01),
        "norm1_g": 1.0 + nrm(ks[6], (L, D), 0.05),
        "norm2_g": 1.0 + nrm(ks[7], (L, D), 0.05),
        "w_in": nrm(ks[8], (L, D, IN_WIDTH), D ** -0.5),
        "conv_w": nrm(ks[9], (L, CONV_K, CONV_W), CONV_K ** -0.5),
        "conv_b": nrm(ks[10], (L, CONV_W), 0.01),
        "conv_ln_g": 1.0 + nrm(ks[11], (L, CONV_W), 0.05),
        "conv_ln_b": nrm(ks[12], (L, CONV_W), 0.01),
        "w_conv_out": nrm(ks[13], (L, CONV_W, D), CONV_W ** -0.5),
        "na_rpb": nrm(ks[14], (L, NA_HEADS, 2 * NA_KH_MAX - 1, 2 * NA_KW - 1), 0.1),
        "w_na_out": nrm(ks[15], (L, NA_W, D), NA_W ** -0.5),
        "q_norm_g": 1.0 + nrm(ks[16], (L, HEAD_DIM), 0.05),
        "k_norm_g": 1.0 + nrm(ks[17], (L, HEAD_DIM), 0.05),
        "w_gqa_out": nrm(ks[18], (L, GQA_Q_W, D), GQA_Q_W ** -0.5),
        "w_out": nrm(ks[19], (L, D, D), D ** -0.5),
        "w_ffn_in": nrm(ks[20], (L, D, 2 * FFN_HIDDEN), D ** -0.5),
        "w_ffn_out": nrm(ks[21], (L, FFN_HIDDEN, D), FFN_HIDDEN ** -0.5),
        "final_g": 1.0 + nrm(ks[22], (D,), 0.05),
    }

def second_block(x, c, ctx, c_ctx, w_mod, b_mod, norm1_g, norm2_g, w_in, conv_w, conv_b, conv_ln_g,
              conv_ln_b, w_conv_out, na_rpb, w_na_out, q_norm_g, k_norm_g, w_gqa_out, w_out,
              w_ffn_in, w_ffn_out, final_g):
    S = x.shape[1]
    t = jnp.arange(S)
    pos_row = (t // GRID_W).astype(jnp.float32)
    pos_col = (t % GRID_W).astype(jnp.float32)
    silu_c = jax.nn.silu(c)
    silu_cc = jax.nn.silu(c_ctx)
    xc = ctx
    for l in range(DEPTH):
        last = l == DEPTH - 1
        sh1, sc1, g1, sh2, sc2, g2 = jnp.split((silu_c @ w_mod[l] + b_mod[l])[:, None, :], 6, axis=-1)
        csh1, csc1, cg1, csh2, csc2, cg2 = jnp.split(silu_cc @ w_mod[l] + b_mod[l], 6, axis=-1)

        h = modulate(rmsnorm_2(x, norm1_g[l]), sh1, sc1)
        hc = modulate(rmsnorm_2(xc, norm1_g[l]), csh1, csc1)
        a, naq, nak, nav, gq, gk, gv, gates = split_in(h @ w_in[l])
        ac, naqc, nakc, navc, gqc, gkc, gvc, gatesc = split_in(hc @ w_in[l])

        na_kc, na_vc = heads(nakc, NA_HEADS), heads(navc, NA_HEADS)
        g_kc = rmsnorm_2(heads(gkc, GQA_KV_HEADS), k_norm_g[l])
        g_vc = heads(gvc, GQA_KV_HEADS)

        br_a = conv_branch(a, conv_w[l], conv_b[l], conv_ln_g[l], conv_ln_b[l], w_conv_out[l])
        br_b = na_latent(heads(naq, NA_HEADS), heads(nak, NA_HEADS), heads(nav, NA_HEADS),
                         na_kc, na_vc, na_rpb[l]) @ w_na_out[l]
        q = axial_rope(rmsnorm_2(heads(gq, GQA_Q_HEADS), q_norm_g[l]), pos_row, pos_col)
        k = axial_rope(rmsnorm_2(heads(gk, GQA_KV_HEADS), k_norm_g[l]), pos_row, pos_col)
        br_c = gqa_latent(q, k, heads(gv, GQA_KV_HEADS), g_kc, g_vc) @ w_gqa_out[l]
        x = x + g1 * merge(br_a, br_b, br_c, gates, w_out[l])
        x = x + g2 * swiglu(modulate(rmsnorm_2(x, norm2_g[l]), sh2, sc2), w_ffn_in[l], w_ffn_out[l])

        if not last:
            cbr_a = conv_branch(ac, conv_w[l], conv_b[l], conv_ln_g[l], conv_ln_b[l], w_conv_out[l])
            cbr_b = dense_attention(heads(naqc, NA_HEADS), na_kc, na_vc) @ w_na_out[l]
            cq = rmsnorm_2(heads(gqc, GQA_Q_HEADS), q_norm_g[l])
            cbr_c = dense_attention(cq, g_kc, g_vc) @ w_gqa_out[l]
            xc = xc + cg1 * merge(cbr_a, cbr_b, cbr_c, gatesc, w_out[l])
            xc = xc + cg2 * swiglu(modulate(rmsnorm_2(xc, norm2_g[l]), csh2, csc2), w_ffn_in[l], w_ffn_out[l])
    return rmsnorm_2(x, final_g)


def setup_inputs(seed=0):
    out = dict(first_inputs(seed))
    for name, value in second_inputs(seed + 1).items():
        if name != "x":
            out[name + "_2"] = value
    return out


def reference(
    x, lru_norm_g, lru_w_in, lru_conv_w, lru_conv_b, lru_gate_w, lru_gate_b, lru_a_param,
    lru_w_out, nsa_norm_g, nsa_w_in, nsa_cmp_pos, nsa_cmp_w1, nsa_cmp_b1, nsa_cmp_w2, nsa_w_out,
    ffn_norm_g, ffn_w_in, ffn_conv_w, ffn_conv_b, ffn_w_out, final_norm_g, c_2, ctx_2, c_ctx_2,
    w_mod_2, b_mod_2, norm1_g_2, norm2_g_2, w_in_2, conv_w_2, conv_b_2, conv_ln_g_2,
    conv_ln_b_2, w_conv_out_2, na_rpb_2, w_na_out_2, q_norm_g_2, k_norm_g_2, w_gqa_out_2,
    w_out_2, w_ffn_in_2, w_ffn_out_2, final_g_2,
):
    x = first_block(
        x, lru_norm_g, lru_w_in, lru_conv_w, lru_conv_b, lru_gate_w, lru_gate_b, lru_a_param,
        lru_w_out, nsa_norm_g, nsa_w_in, nsa_cmp_pos, nsa_cmp_w1, nsa_cmp_b1, nsa_cmp_w2,
        nsa_w_out, ffn_norm_g, ffn_w_in, ffn_conv_w, ffn_conv_b, ffn_w_out, final_norm_g,
    )
    return second_block(
        x, c_2, ctx_2, c_ctx_2, w_mod_2, b_mod_2, norm1_g_2, norm2_g_2, w_in_2, conv_w_2,
        conv_b_2, conv_ln_g_2, conv_ln_b_2, w_conv_out_2, na_rpb_2, w_na_out_2, q_norm_g_2,
        k_norm_g_2, w_gqa_out_2, w_out_2, w_ffn_in_2, w_ffn_out_2, final_g_2,
    )


_drawn_inputs = setup_inputs


def setup_inputs(seed=0):
    import zlib

    import numpy as np

    out = dict(_drawn_inputs(seed))
    spreads = {}
    factors = {'lru_gate_b': 3.116,
     'nsa_cmp_b1': 8.0,
     'ffn_conv_b': 3.666,
     'b_mod_2': 4.288,
     'norm1_g_2': 6.2,
     'norm2_g_2': 2.696,
     'conv_b_2': 8.0,
     'conv_ln_g_2': 6.082,
     'conv_ln_b_2': 8.0,
     'na_rpb_2': 8.0,
     'q_norm_g_2': 8.0,
     'k_norm_g_2': 8.0}
    for name, (base, spread) in spreads.items():
        noise = np.random.default_rng([zlib.crc32(name.encode()), seed]).standard_normal(out[name].shape)
        drawn = base * np.exp(spread * noise) if base else spread * noise
        out[name] = __import__('jax').numpy.asarray(drawn.astype(out[name].dtype))
    for name, factor in factors.items():
        out[name] = (out[name] * factor).astype(out[name].dtype)
    return out
```

```python
import numpy as np

import concourse.bass as bass
from concourse import mybir
from contextlib import ExitStack

F32 = mybir.dt.float32
ALU = mybir.AluOpType
ACT = mybir.ActivationFunctionType
AX = mybir.AxisListType.X

P = 128
D = 1024
KD = D // P
S = 256
S2 = 2 * S
EPS = 1e-6
LRU = 1280
KL = LRU // P
CONV_L = 4
FF1 = 3072
KF1 = FF1 // P
CONV_F = 3
HEADS = 16
DH = 64
KV = 4
GROUP = HEADS // KV
CMP_BLOCK, CMP_STRIDE = 32, 16
NCMP = (S - CMP_BLOCK) // CMP_STRIDE + 1
CMPW = 32
HID = 256
CW = 512
KC = CW // P
CONV_K = 31
HALO = CONV_K // 2
FF2 = 2816
KF2 = FF2 // P
GRID = 64
NEG = -1e30

TILES = 32
HALF = TILES // 2
RING = 4
DEPTH = 2


def columns(parts):
    at, where = 0, {}
    for name, n in parts:
        where[name] = at
        at += n
    where["end"] = at
    return where


PARAM = columns([
    ("lru_g", KD), ("nsa_g", KD), ("ffn_g", 2 * KD), ("final_g", KD), ("norm1", 2 * KD), ("norm2", 2 * KD),
    ("final2", KD), ("lru_cw", KL * CONV_L), ("lru_cb", KL), ("gate_b", 2 * KL), ("a_param", KL),
    ("ffn_cw", 2 * KF1 * CONV_F), ("ffn_cb", 2 * KF1), ("cmp_b1", 4), ("cmp_pos", 2 * HALF),
    ("b_mod", 2 * 48), ("conv_w", 2 * KC * CONV_K), ("conv_b", 2 * KC), ("ln_g", 2 * KC), ("ln_b", 2 * KC),
    ("q_g", 2), ("k_g", 2), ("c", 2 * KD), ("w2k", 2 * P), ("w2v", 2 * DH),
])
CONST = columns([
    ("ident", P), ("ones", P), ("heads1", P), ("rope", P), ("cos", S), ("sin", S), ("causal", 2 * S),
    ("cmp_bias", 2 * HEADS * NCMP), ("cmp_mask", 2 * NCMP), ("na_mask", GRID),
])

FULL = (HALF, HALF)
STREAM = [("lru_in", 5, FULL), ("lru_gate", 1, (16, 4)), ("mod0", 12, FULL), ("lru_out", 3, (16, 1)),
          ("ffn_in0", 12, FULL), ("ffn_out0", 6, FULL), ("nsa_q", 2, FULL), ("nsa_kv", 4, FULL),
          ("nsa_v", 1, FULL), ("nsa_gate", 1, (8, 1)), ("cmp", 2, FULL), ("mod1", 12, FULL),
          ("nsa_out", 2, FULL), ("ffn_in1", 12, FULL), ("ffn_out1", 6, FULL)]
for _l in range(DEPTH):
    STREAM += [(f"in{_l}", 6, FULL), (f"in_gkv{_l}", 1, (16, 8))]
    for _b in range(3):
        STREAM += [(f"gates{_l}{_b}", 2, FULL), (f"branch{_l}{_b}", 1, FULL)]
    STREAM += [(f"out{_l}", 2, FULL), (f"mlp_in{_l}", 11, FULL), (f"mlp_out{_l}", 6, (16, 1))]
FIRST_UNIT, PARTIAL, _n = {}, {}, 0
for _name, _units, _halves in STREAM:
    FIRST_UNIT[_name] = _n
    _n += _units
    if _halves != FULL:
        PARTIAL[_n - 1] = _halves
UNITS = _n

BANKS = [("lru_in", (5, 5, 5, 5)), ("lru_gate", (3, 3, 2, 2)), ("mod0", (0, 0, 0, 12)), ("lru_out", (2,) * 4),
         ("ffn_in0", (12,) * 4), ("ffn_out0", (2,) * 4), ("nsa_q", (2,) * 4), ("nsa_kv", (4,) * 4),
         ("nsa_v", (1, 1, 0, 0)), ("nsa_gate", (0, 0, 1, 1)), ("cmp", (1,) * 4), ("mod1", (0, 0, 0, 12)),
         ("cmp2", (1, 1, 0, 0)), ("nsa_out", (2,) * 4), ("ffn_in1", (12,) * 4), ("ffn_out1", (2,) * 4)]
for _l in range(DEPTH):
    BANKS += [(f"conv_in{_l}", (2,) * 4), (f"naq{_l}", (1,) * 4), (f"nak{_l}", (1,) * 4), (f"nav{_l}", (1,) * 4),
              (f"gq{_l}", (1,) * 4), (f"gkv{_l}", (1,) * 4)]
    for _b in range(3):
        BANKS += [(f"gates{_l}{_b}", (2,) * 4), (f"branch{_l}{_b}", (2,) * 4)]
    BANKS += [(f"out{_l}", (2,) * 4), (f"mlp_in{_l}", (11,) * 4), (f"mlp_out{_l}", (2,) * 4)]
USED, _c = {}, [0, 0, 0, 0]
for _name, _uses in BANKS:
    USED[_name] = list(_c)
    _c = [a + b for a, b in zip(_c, _uses)]


class Count:

    def __init__(self, base=0):
        self.base, self.k, self.per, self.n = base, 0, 0, None

    def next(self, k=1):
        if self.n is None:
            self.base += k
            return self.base
        self.k += k
        return self.n * self.per + (self.base + self.k)

    def enter(self, per):
        self.per = per

    def at(self, n):
        self.n, self.k = n, 0

    def leave(self, steps):
        assert self.k == self.per, (self.k, self.per)
        self.base += self.per * steps
        self.n = None


def steps(eng, count, *counts):
    for c, per in counts:
        c.enter(per)
    turns = count // RING
    with eng.Fori(0, turns) as i:
        for j in range(RING):
            n = i * RING + j
            for c, _ in counts:
                c.at(n)
            yield n, j, i
    for j in range(count - turns * RING):
        n = turns * RING + j
        for c, _ in counts:
            c.at(n)
        yield n, j, turns
    for c, _ in counts:
        c.leave(count)


def attention_jobs(kind, layer):
    if kind == "nsa":
        return [(t, par, q) for t in range(HEADS // 2) for q in range(2) for par in range(2)]
    tiles = 4 if layer == 0 else 2
    return [(t, par, q) for t in range(4) for q in range(tiles) for par in range(2)]


def key_blocks(kind, q):
    if kind == "nsa":
        return list(range(q + 1))
    return [0, 1, 2, 3] if q < 2 else [2, 3]


def program(nc, wstream, params_in, consts_in, rpb_in, x_in, out):
    ctx = ExitStack()
    with ctx:
        def sb(name, shape):
            return ctx.enter_context(nc.sbuf_tensor(name, shape, F32))

        def sem(name):
            return ctx.enter_context(nc.semaphore(name))

        ring = sb("ring", [P, RING, TILES * P])
        x = sb("x", [P, KD, S2])
        h = sb("h", [P, KD, S2])
        prm = sb("prm", [P, PARAM["end"]])
        cst = sb("cst", [P, CONST["end"]])
        rs = sb("rs", [P, S2])
        small = sb("small", [P, 320])
        mods = sb("mods", [P, 2, 48, 2])
        mrow = sb("mrow", [P, 512])
        gn = sb("gn", [P, 2, 2, KD])
        arena = sb("arena", [P, 23600])

        def part(at, *shape):
            n = int(np.prod(shape))
            assert at + n <= 23600, at + n
            a = arena[:, at:at + n]
            if len(shape) == 2:
                a = a.rearrange("p (a b) -> p a b", b=shape[1])
            if len(shape) == 3:
                a = a.rearrange("p (a b c) -> p a b c", b=shape[1], c=shape[2])
            return a

        def par(name, i=0, n=1):
            return prm[:, PARAM[name] + i:PARAM[name] + i + n]

        def con(name, i, n):
            return cst[:, CONST[name] + i:CONST[name] + i + n]

        ident, ones, heads1, rope = (con(n, 0, P) for n in ("ident", "ones", "heads1", "rope"))

        l_y, l_x, l_r, l_i, l_b, l_t = (part(i * KL * S, KL, S) for i in range(6))
        f_hid = part(0, KF1, S)
        f_conv, f_gelu = part(KF1 * S, 2, S), part(KF1 * S + 2 * S, 2, S)
        m_hid = part(0, KF2, S2)
        m_silu = part(KF2 * S2, 2, S2)
        n_q = part(0, KD, S)
        n_kc = part(2048, 2, KV, S)
        n_k = part(4096, 2, KV, S)
        n_v = part(6144, 2, 512)
        n_gate = part(7168, 2, 48)
        n_blk = part(7264, 32, KV * NCMP)
        n_hid = part(9184, 4, KV * CMPW)
        n_ck = part(9696, 1, KV * NCMP)
        n_cv = part(9760, KV, DH)
        n_vz = part(10016, HEADS, DH)
        n_pc = part(11040, 2, HEADS * CMPW)
        n_pcT = part(12064, 2, KV, P)
        n_hv = part(13088, 2 * KV, P)
        a_u = part(0, 2 * KC, S + 2 * HALO)
        a_u3 = a_u.rearrange("p (c s) t -> p c s t", s=2)
        a_cy = part(2304, KC, S2)
        a_naq, a_nak, a_nav = (part(4352 + 2048 * i, 4, S2) for i in range(3))
        a_gq = part(10496, 4, S2)
        a_gk = part(12544, 2, S2)
        a_gv = part(13568, 4, P)
        a_rpb = part(14080, 8 * 6, GRID)
        a_y = part(17152, KD, S2)
        a_sig = part(6400, KD, S2)
        s_p = part(21248, 2, S2)
        s_pT = part(22272, 2, S2)
        s_cm = small[:, 0:16]
        s_cs = small[:, 16:32]
        s_cr = small[:, 32:48]
        s_max = small[:, 48:56]
        s_sum = small[:, 56:64]
        s_rec = small[:, 64:72]
        soft = small[:, 72:82]
        sgn = small[:, 82:92]
        sca = small[:, 92:132]
        silc = small[:, 132:148].rearrange("p (k s) -> p k s", s=2)

        ps = [ctx.enter_context(nc.psum_tensor(f"ps{i}", [P, 512], F32)) for i in range(8)]
        acc, psS, psT, psO = ps[0:4], ps[4:6], ps[6], ps[7]
        cmp_banks = (psS, (psT, psO))

        landed = [[sem(f"landed{s}{hh}") for hh in range(2)] for s in range(RING)]
        slot_used = sem("slot_used")
        params_landed, x_landed, rpb_landed, ctx_landed = sem("params_landed"), sem("x_landed"), sem("rpb_landed"), sem("ctx_landed")
        acc_full = [sem(f"acc_full{b}") for b in range(4)]
        acc_free = [sem(f"acc_free{b}") for b in range(4)]
        squares_ready, sums_ready, inverse_ready, root_ready = (sem(n) for n in ("squares_ready", "sums_ready", "inverse_ready", "root_ready"))
        scaled_ready, h_ready = sem("scaled_ready"), sem("h_ready")
        act_tile_ready = sem("act_tile_ready")
        dve_tile_ready = sem("dve_tile_ready")
        silu_ready, mod_turned, mod_taken = sem("silu_ready"), sem("mod_turned"), sem("mod_taken")
        pe_aux_full, pe_aux_free = sem("pe_aux_full"), sem("pe_aux_free")
        operand_ready = sem("operand_ready")
        act_operand_ready = sem("act_operand_ready")
        score_full, score_max, prob_exp, prob_ready = (sem(n) for n in ("score_full", "score_max", "prob_exp", "prob_ready"))
        turned_full, turned_ready, o_full, o_free = (sem(n) for n in ("turned_full", "turned_ready", "o_full", "o_free"))
        dve_step, act_step, pool_step = sem("dve_step"), sem("act_step"), sem("pool_step")
        rpb_ready, rpb_place = sem("rpb_ready"), sem("rpb_place")
        conv_done, ln_summed = sem("conv_done"), sem("ln_summed")
        mrow_zero = sem("mrow_zero")
        decay_ready, pads_ready, first_done = sem("decay_ready"), sem("pads_ready"), sem("first_done")
        rotated, centred = sem("rotated"), sem("centred")
        out_ready, out_stored = sem("out_ready"), sem("out_stored")

        block = ctx.enter_context(nc.Block())

        @block.sync
        def _(sp):
            sp.dma_start(x[:, :, 0:S], x_in[:, :, 0:S]).then_inc(x_landed, 16)
            sp.dma_start(prm[:], params_in).then_inc(params_landed, 16)
            sp.dma_start(cst[:], consts_in).then_inc(params_landed, 16)

            def load(u, slot, halves=FULL):
                for hh in range(2):
                    a = hh * HALF * P
                    b = a + halves[hh] * P
                    src = wstream[u:u + 1, :, a:b] if isinstance(u, int) else wstream[bass.ds(u, 1), :, a:b]
                    sp.dma_start(ring[:, slot, a:b], src.rearrange("u p n -> (u p) n")).then_inc(landed[slot][hh], 16)

            u = 0
            while u < UNITS:
                e = u
                while e + RING <= UNITS and not any(v in PARTIAL for v in range(e, e + RING)):
                    e += RING
                if e - u >= 2 * RING and u >= RING:
                    with sp.Fori(0, (e - u) // RING) as i:
                        for j in range(RING):
                            sp.wait_ge(slot_used, i * RING + (u + j - RING + 1))
                            load(i * RING + (u + j), (u + j) % RING)
                    u = e
                    continue
                if u >= RING:
                    sp.wait_ge(slot_used, u - RING + 1)
                load(u, u % RING, PARTIAL.get(u, FULL))
                u += 1
                if u == 2:
                    sp.dma_start(x[:, :, S:S2], x_in[:, :, S:S2]).then_inc(ctx_landed, 16)
            for slot in range(RING):
                for hh in range(2):
                    sp.wait_ge(landed[slot][hh], 16 * len(range(slot, UNITS, RING)))
            for k in range(KD):
                sp.wait_ge(out_ready, k + 1)
                sp.dma_start(out[:, k, :], h[:, k, 0:S]).then_inc(out_stored, 16)
            sp.wait_ge(out_stored, 16 * KD)

        @block.gpsimd
        def _(pool):
            nc.gpsimd.memset(mrow[:], 0.0).then_inc(mrow_zero, 1)
            for l in range(DEPTH):
                pool.wait_ge(rpb_place, l + 1)
                pool.dma_start(a_rpb.rearrange("p a b -> p (a b)"), rpb_in[l]).then_inc(rpb_landed, 16)
                pool.wait_ge(rpb_landed, 16 * (l + 1))
                nc.gpsimd.tensor_tensor(a_rpb, a_rpb, con("na_mask", 0, GRID).unsqueeze(1).broadcast_to([P, 48, GRID]),
                                        ALU.add).then_inc(rpb_ready, 1)

        @block.tensor
        def _(pe):
            state = {"release": False}
            squares, hr, taken = Count(), Count(), Count()
            oper, aoper = Count(), Count()
            prob_c, ofree_c = Count(), Count()

            def mm(*a, **k):
                ins = nc.tensor.matmul(*a, **k)
                if state["release"]:
                    ins.then_inc(slot_used, 1)
                    state["release"] = False
                return ins

            def unit(name, i, turn=0):
                u = FIRST_UNIT[name] + i
                slot, use = u % RING, turn + (u // RING + 1)

                def tile(t, n=1):
                    if t % HALF == 0:
                        pe.wait_ge(landed[slot][t // HALF], use * 16)
                    return ring[:, slot, t * P:(t + n) * P]
                return tile

            def done_unit():
                state["release"] = True

            def flush(ins):
                if state["release"]:
                    ins.then_inc(slot_used, 1)
                    state["release"] = False

            def free(stage, b, n):
                pe.wait_ge(acc_free[b], n + USED[stage][b])

            def norm(N):
                for k in range(KD):
                    pe.wait_ge(squares_ready, squares.next())
                    ins = nc.tensor.matmul(psO[:, 0:N], ones, h[:, k, 0:N], start=k == 0, stop=k == KD - 1)
                ins.then_inc(sums_ready, 1)

            def gemm_group(stage, w, n, N=S, first=0):
                for m in range(4):
                    free(stage, m, n)
                    for k in range(KD):
                        if first and m == 0:
                            pe.wait_ge(h_ready, hr.next(first))
                        ins = mm(acc[m][:, 0:N], w(m * KD + k), h[:, k, 0:N], start=k == 0, stop=k == KD - 1)
                    ins.then_inc(acc_full[m], 1)

            def hidden_out(stage, chunks, src, N, ready):
                w = None
                for m in range(KD):
                    free(stage, m % 4, m // 4)
                    for k in range(chunks):
                        t = m * chunks + k
                        if t % TILES == 0:
                            if t:
                                done_unit()
                            w = unit(stage, t // TILES)
                        if m == 0:
                            ready(k)
                        ins = mm(acc[m % 4][:, 0:N], w(t % TILES), src[:, k, 0:N], start=k == 0, stop=k == chunks - 1)
                    ins.then_inc(acc_full[m % 4], 1)
                done_unit()

            def modulation(l):
                stage = f"mod{l}"

                if l == 0:
                    pe.wait_ge(silu_ready, 1)
                assert state["release"]
                for n, j, i in steps(pe, 12, (taken, 1)):
                    w = unit(stage, j, i)
                    free(stage, 3, n)
                    for k in range(KD):
                        ins = mm(acc[3][0:2, :], silc[:, k, :], w(4 * k, 4), start=k == 0, stop=k == KD - 1)
                    ins.then_inc(acc_full[3], 1)
                    done_unit()
                    pe.wait_ge(acc_free[3], n + (USED[stage][3] + 1))
                    pe.wait_ge(mod_taken, taken.next() - 1)
                    for q in range(4):
                        ins = nc.tensor.transpose(psT[:, q * P:(q + 1) * P], mrow[:, q * P:(q + 1) * P], ident)
                    ins.then_inc(mod_turned, 1)

            def softmax(kind, layer):
                jobs = attention_jobs(kind, layer)
                for j in range(len(jobs) + 2):
                    if j < len(jobs):
                        t, p, q = jobs[j]
                        rows_ = slice(DH * p, DH * p + DH)
                        qs = slice(q * P, (q + 1) * P)
                        if j >= 2:
                            pe.wait_ge(prob_exp, prob_c.base + j - 1)
                        if kind == "nsa":
                            g, nk = (2 * t + p) // GROUP, (q + 1) * P
                            for br in range(2):
                                ins = mm(psS[j % 2][:, br * nk:(br + 1) * nk], n_q[rows_, t, qs], n_k[rows_, br, g, 0:nk],
                                         start=True, stop=True)
                        else:
                            a = 0 if q < 2 else S
                            key = a_nak[rows_, t, a:S2] if kind == "na" else a_gk[rows_, t // 2, a:S2]
                            qq = (a_naq if kind == "na" else a_gq)[rows_, t, qs]
                            ins = mm(psS[j % 2][:, 0:S2 - a], qq, key, start=True, stop=True)
                        ins.then_inc(score_full, 1)
                    if 1 <= j <= len(jobs):
                        t, p, q = jobs[j - 1]
                        nb = len(key_blocks(kind, q)) * (2 if kind == "nsa" else 1)
                        pe.wait_ge(prob_ready, prob_c.base + j)
                        if j >= 2:
                            pe.wait_ge(turned_ready, prob_c.base + j - 1)
                        for b in range(nb):
                            ins = nc.tensor.transpose(psT[:, b * P:(b + 1) * P], s_p[:, (j - 1) % 2, b * P:(b + 1) * P], ident)
                        ins.then_inc(turned_full, 1)
                    if j >= 2:
                        t, p, q = jobs[j - 2]
                        o = psO[DH * p:DH * p + DH, 0:P]
                        blocks = key_blocks(kind, q)
                        head = 2 * t + p
                        if p == 0:
                            pe.wait_ge(o_free, ofree_c.base + (j - 2) // 2)
                        pe.wait_ge(turned_ready, prob_c.base + j - 1)
                        pT = s_pT[:, (j - 2) % 2, :]
                        terms = []
                        if kind == "nsa":
                            g = head // GROUP
                            terms.append((n_vz[:, head, :], n_pcT[:, q, g, :]))
                            for br in range(2):
                                for b in blocks:
                                    i = br * len(blocks) + b
                                    terms.append((n_v[:, b, (br * KV + g) * DH:(br * KV + g + 1) * DH], pT[:, i * P:(i + 1) * P]))
                        else:
                            for i, b in enumerate(blocks):
                                v = a_nav[:, b, head * DH:(head + 1) * DH] if kind == "na" else a_gv[:, b, (t // 2) * DH:(t // 2 + 1) * DH]
                                terms.append((v, pT[:, i * P:(i + 1) * P]))
                        for i, (v, pr) in enumerate(terms):
                            ins = mm(o, v, pr, start=i == 0, stop=i == len(terms) - 1)
                        ins.then_inc(o_full, 1)
                prob_c.base += len(jobs)
                ofree_c.base += len(jobs) // 2

            pe.wait_ge(params_landed, 32)

            norm(S)
            for n in range(5):
                w = unit("lru_in", n)
                gemm_group("lru_in", w, n, first=int(n == 0))
                done_unit()
            w = unit("lru_gate", 0)
            for n in range(KL):
                b = n % 4
                free("lru_gate", b, n // 4)
                pe.wait_ge(acc_free[2 + n % 2], USED["lru_in"][2 + n % 2] + n // 2 + 1)
                mm(acc[b][:, 0:S], w(2 * n), l_x[:, n, :], start=True, stop=True)
                mm(acc[b][:, S:S2], w(2 * n + 1), l_x[:, n, :], start=True, stop=True).then_inc(acc_full[b], 1)
            done_unit()
            modulation(0)
            hidden_out("lru_out", KL, l_y, S, lambda k: pe.wait_ge(operand_ready, oper.next()))

            def ffn(l):
                norm(S)
                for k in range(KD):
                    pe.wait_ge(h_ready, hr.next())
                assert state["release"]
                for n, j, i in steps(pe, 12):
                    w = unit(f"ffn_in{l}", j, i)
                    gemm_group(f"ffn_in{l}", w, n)
                    done_unit()
                st = f"ffn_in{l}"
                hidden_out(f"ffn_out{l}", KF1, f_hid, S,
                           lambda k: pe.wait_ge(acc_free[2 + k % 2], USED[st][2 + k % 2] + k // 2 + 1))

            ffn(0)

            norm(S)
            for n in range(2):
                gemm_group("nsa_q", unit("nsa_q", n), n, first=int(n == 0))
                done_unit()
            for n in range(4):
                gemm_group("nsa_kv", unit("nsa_kv", n), n)
                done_unit()
            w = unit("nsa_v", 0)
            for q in range(2):
                free("nsa_v", q, 0)
                for k in range(KD):
                    ins = mm(acc[q][:], h[:, k, q * P:(q + 1) * P], w(4 * k, 4), start=k == 0, stop=k == KD - 1)
                ins.then_inc(acc_full[q], 1)
            done_unit()
            w = unit("nsa_gate", 0)
            for q in range(2):
                free("nsa_gate", 2 + q, 0)
                for k in range(KD):
                    ins = mm(acc[2 + q][:, 0:48], h[:, k, q * P:(q + 1) * P], w(k)[:, 0:48], start=k == 0, stop=k == KD - 1)
                ins.then_inc(acc_full[2 + q], 1)
            done_unit()
            for kv in range(2):
                w = unit("cmp", kv)
                pe.wait_ge(operand_ready, oper.next())
                for m in range(2):
                    free("cmp", 2 * kv + m, 0)
                    for jj in range(HALF):
                        ins = mm(acc[2 * kv + m][:, 0:KV * NCMP], w(m * HALF + jj), n_blk[:, kv * HALF + jj, :], start=jj == 0, stop=jj == HALF - 1)
                    ins.then_inc(acc_full[2 * kv + m], 1)
                done_unit()
            modulation(1)
            for m in range(2):
                pe.wait_ge(acc_free[m], USED["cmp"][m] + 1)
            free("cmp2", 0, 0)
            for m in range(2):
                ins = mm(acc[0][:, 0:KV * NCMP], par("w2k", m * P, P), n_hid[:, m, :].rearrange("p (g c) -> p g c", c=CMPW)[:, :, 0:NCMP],
                         start=m == 0, stop=m == 1)
            ins.then_inc(acc_full[0], 1)
            pe.wait_ge(operand_ready, oper.next())
            free("cmp2", 1, 0)
            for g in range(KV):
                for m in range(2):
                    ins = mm(acc[1][:, g * DH:(g + 1) * DH], n_hv[:, m * KV + g, :], par("w2v", m * DH, DH), start=m == 0, stop=m == 1)
            ins.then_inc(acc_full[1], 1)
            pe.wait_ge(acc_free[0], USED["cmp2"][0] + 1)
            pe.wait_ge(acc_free[1], USED["cmp2"][1] + 1)
            for q in range(2):
                for head in range(HEADS):
                    t, p, g = head // 2, head % 2, head // GROUP
                    r_ = slice(DH * p, DH * p + DH)
                    ins = mm(cmp_banks[q][p][:, t * NCMP:(t + 1) * NCMP], n_q[r_, t, q * P:(q + 1) * P], n_ck[r_, 0, g * NCMP:(g + 1) * NCMP],
                             start=True, stop=True)
                ins.then_inc(pe_aux_full, 1)
            pe.wait_ge(operand_ready, oper.next(2))
            for q in range(2):
                for g in range(KV):
                    ins = nc.tensor.transpose((psT, psO)[q][:, g * P:(g + 1) * P], n_pc[:, q, g * P:(g + 1) * P], ident)
                ins.then_inc(pe_aux_full, 1)
            pe.wait_ge(pe_aux_free, 2)
            softmax("nsa", 0)
            pe.wait_ge(o_free, ofree_c.base)
            hidden_out("nsa_out", KD, n_q, S, lambda k: None)

            ffn(1)

            def dual(l):
                N = S2 if l == 0 else S
                norm(S2)
                for n in range(2):
                    gemm_group(f"conv_in{l}", unit(f"in{l}", n), n, first=2 * int(n == 0), N=N)
                    done_unit()
                gemm_group(f"naq{l}", unit(f"in{l}", 2), 0, N=N)
                done_unit()
                gemm_group(f"nak{l}", unit(f"in{l}", 3), 0, N=S2)
                done_unit()
                w = unit(f"in{l}", 4)
                for q in range(4):
                    free(f"nav{l}", q, 0)
                    for k in range(KD):
                        ins = mm(acc[q][:], h[:, k, q * P:(q + 1) * P], w(4 * k, 4), start=k == 0, stop=k == KD - 1)
                    ins.then_inc(acc_full[q], 1)
                done_unit()
                gemm_group(f"gq{l}", unit(f"in{l}", 5), 0, N=N)
                done_unit()
                w = unit(f"in_gkv{l}", 0)
                for m in range(2):
                    free(f"gkv{l}", m, 0)
                    for k in range(KD):
                        ins = mm(acc[m][:], w(m * KD + k), h[:, k, :], start=k == 0, stop=k == KD - 1)
                    ins.then_inc(acc_full[m], 1)
                for m in range(2):
                    free(f"gkv{l}", 2 + m, 0)
                    for e in range(2):
                        for k in range(KD):
                            q = 2 * m + e
                            ins = mm(acc[2 + m][:, e * P:(e + 1) * P], h[:, k, q * P:(q + 1) * P], w(2 * KD + k), start=k == 0, stop=k == KD - 1)
                    ins.then_inc(acc_full[2 + m], 1)
                done_unit()
                for c in range(6):
                    n = N if c < 4 else S2
                    src = a_gq[:, c, :] if c < 4 else a_gk[:, c - 4, :]
                    pe.wait_ge(act_operand_ready, aoper.next())
                    nc.tensor.matmul(psS[0][:, 0:n], heads1, s_p[:, 0, 0:n], start=True, stop=True).then_inc(pe_aux_full, 1)
                    pe.wait_ge(operand_ready, oper.next())
                    nc.tensor.matmul(psS[1][:, 0:S], rope, src[:, 0:S], start=True, stop=True).then_inc(pe_aux_full, 1)
                pe.wait_ge(conv_done, KC * (l + 1))
                for c in range(KC):
                    ins = mm(psT[:, 0:N], ones, a_cy[:, c, 0:N], start=c == 0, stop=c == KC - 1)
                ins.then_inc(pe_aux_full, 1)
                for c in range(KC):
                    pe.wait_ge(act_operand_ready, aoper.next())
                    mm(psO[:, 0:N], ones, s_p[:, c % 2, 0:N], start=c == 0, stop=c == KC - 1).then_inc(ln_summed, 1)
                pe.wait_ge(rotated, 6 * (l + 1))
                pe.wait_ge(centred, 2 * KC * (l + 1))
                pe.wait_ge(acc_free[3], USED[f"gkv{l}"][3] + 1)
                pe.wait_ge(acc_free[1], USED[f"gkv{l}"][1] + 1)
                softmax("gqa", l)
                pe.wait_ge(rpb_ready, l + 1)
                softmax("na", l)
                pe.wait_ge(o_free, ofree_c.base)
                for br in range(3):
                    src = (a_cy, a_naq, a_gq)[br]
                    for n in range(2):
                        gemm_group(f"gates{l}{br}", unit(f"gates{l}{br}", n), n, N=N)
                        done_unit()
                    w = unit(f"branch{l}{br}", 0)
                    if br == 0:
                        pe.wait_ge(act_operand_ready, aoper.next(KC))
                    for m in range(KD):
                        free(f"branch{l}{br}", m % 4, m // 4)
                        for k in range(KC):
                            ins = mm(acc[m % 4][:, 0:N], w(m * KC + k), src[:, k, 0:N], start=k == 0, stop=k == KC - 1)
                        ins.then_inc(acc_full[m % 4], 1)
                    done_unit()
                st = f"branch{l}2"
                hidden_out(f"out{l}", KD, a_y, N, lambda k: pe.wait_ge(acc_free[k % 4], USED[st][k % 4] + k // 4 + 1))
                norm(N)
                for k in range(KD):
                    pe.wait_ge(h_ready, hr.next(N // S))
                assert state["release"]
                for n, j, i in steps(pe, 11):
                    gemm_group(f"mlp_in{l}", unit(f"mlp_in{l}", j, i), n, N=N)
                    done_unit()
                st2 = f"mlp_in{l}"
                hidden_out(f"mlp_out{l}", KF2, m_hid, N, lambda k: pe.wait_ge(acc_free[2 + k % 2], USED[st2][2 + k % 2] + k // 2 + 1))

            norm(S)
            for l in range(DEPTH):
                dual(l)
            norm(S)

        @block.scalar
        def _(act):
            inv, tiles, scaled, jobs_done = Count(), Count(), Count(), Count()
            rot, cen = Count(), Count()

            def full(stage, b, n):
                act.wait_ge(acc_full[b], n + (USED[stage][b] + 1))

            def freed(stage, b, n):
                act.wait_ge(acc_free[b], n + (USED[stage][b] + 1))

            def go(o, i, f, **k):
                return nc.scalar.activation(o, i, f, **k)

            def root_of(N, scale=1.0):
                act.wait_ge(inverse_ready, inv.next())
                go(rs[:, 0:N], rs[:, 0:N], ACT.Sqrt, scale=scale).then_inc(root_ready, 1)

            def norm(N, ready):
                for k in range(KD):
                    ready(k)
                    go(h[:, k, 0:N], x[:, k, 0:N], ACT.Square).then_inc(squares_ready, 1)
                root_of(N)

            def after(stage):
                return lambda k: freed(stage, k % 4, k // 4)

            def copy(stage, b, n, o, i, func=ACT.Copy, **k):
                full(stage, b, n)
                go(o, i, func, **k).then_inc(acc_free[b], 1)

            def mod_row(l, n):
                copy(f"mod{l}", 3, n, mrow[0:2, :], acc[3][0:2, :])

            act.wait_ge(params_landed, 32)
            act.wait_ge(x_landed, 16)
            norm(S, lambda k: None)
            act.wait_ge(dve_tile_ready, tiles.next())
            go(sca[:, 0:10], sca[:, 0:10], ACT.Exp).then_inc(act_tile_ready, 1)
            go(silc.rearrange("p k s -> p (k s)"), par("c", 0, 2 * KD), ACT.Silu).then_inc(silu_ready, 1)
            for n in range(5):
                for j in range(2):
                    copy("lru_in", j, n, l_y[:, 2 * n + j, :], acc[j][:, 0:S], func=ACT.Gelu_apprx_tanh)
            for n in range(KL):
                b = n % 4
                full("lru_gate", b, n // 4)
                go(l_r[:, n, :], acc[b][:, 0:S], ACT.Sigmoid, bias=par("gate_b", n))
                go(l_i[:, n, :], acc[b][:, S:S2], ACT.Sigmoid, bias=par("gate_b", KL + n)).then_inc(acc_free[b], 1)
            act.wait_ge(decay_ready, 1)
            act.wait_ge(mrow_zero, 1)
            freed("lru_gate", 1, 2)
            for n in range(KL):
                go(l_b[:, n, :], l_r[:, n, :], ACT.Exp, scale=sca[:, 20 + n:21 + n])
                go(l_t[:, n, :], l_r[:, n, :], ACT.Tanh, scale=sca[:, 30 + n:31 + n]).then_inc(act_tile_ready, 1)
                if n % 3 == 2:
                    mod_row(0, n // 3)
            for n in range(KL):
                act.wait_ge(dve_tile_ready, tiles.next())
                go(l_t[:, n, :], l_t[:, n, :], ACT.Sqrt, scale=2.0).then_inc(act_tile_ready, 1)
                if n < 9:
                    mod_row(0, 3 + n)

            def ffn(l, before):
                norm(S, after(before))
                st = f"ffn_in{l}"
                for n, j, i in steps(act, 12):
                    for e in range(2):
                        freed(st, e, n)
                        act.wait_ge(acc_free[2 + e], n + USED[st][2 + e])
                        go(f_gelu[:, e, :], f_conv[:, e, :], ACT.Gelu_apprx_tanh).then_inc(act_tile_ready, 1)

            def softmax(kind, layer):
                jobs = attention_jobs(kind, layer)
                base = jobs_done.base
                parts = 2 if kind == "nsa" else 1
                for j in range(len(jobs) + 2):
                    if j < len(jobs):
                        t, p, q = jobs[j]
                        nk = len(key_blocks(kind, q)) * P
                        act.wait_ge(score_max, base + j + 1)
                        if j >= 2:
                            act.wait_ge(turned_full, base + j - 1)
                        for br in range(parts):
                            i = (j % 2) * 2 + br
                            ins = go(s_p[:, j % 2, br * nk:(br + 1) * nk], psS[j % 2][:, br * nk:(br + 1) * nk], ACT.Exp,
                                     bias=s_max[:, i:i + 1], accum_out=s_sum[:, i:i + 1])
                        ins.then_inc(prob_exp, 1)
                    if 1 <= j <= len(jobs):
                        t, p, q = jobs[j - 1]
                        n = len(key_blocks(kind, q)) * P * parts
                        act.wait_ge(turned_full, base + j)
                        if j >= 3:
                            act.wait_ge(o_full, base + j - 2)
                        go(s_pT[:, (j - 1) % 2, 0:n], psT[:, 0:n], ACT.Copy).then_inc(turned_ready, 1)
                    if j >= 2 and j % 2 == 1:
                        t, p, q = jobs[j - 2]
                        act.wait_ge(o_full, base + j - 1)
                        o = {"nsa": n_q, "na": a_naq, "gqa": a_gq}[kind]
                        go(o[:, t, q * P:(q + 1) * P], psO[:, 0:P], ACT.Copy).then_inc(o_free, 1)
                jobs_done.base += len(jobs)

            ffn(0, "lru_out")
            norm(S, after("ffn_out0"))
            for n in range(2):
                for m in range(4):
                    copy("nsa_q", m, n, n_q[:, 4 * n + m, :], acc[m][:, 0:S], scale=DH ** -0.5)
            for n in range(2, 4):
                for m in range(4):
                    copy("nsa_kv", m, n, n_k[:, n - 2, m, :], acc[m][:, 0:S])
            for q in range(2):
                copy("nsa_v", q, 0, n_v[:, q, :], acc[q][:])
            for q in range(2):
                copy("nsa_gate", 2 + q, 0, n_gate[:, q, :], acc[2 + q][:, 0:48], func=ACT.Sigmoid)
            act.wait_ge(pads_ready, 1)
            for i in range(4):
                copy("cmp", i, 0, n_hid[:, i, :].rearrange("p (g c) -> p g c", c=CMPW)[:, :, 0:NCMP],
                     acc[i][:, 0:KV * NCMP].rearrange("p (g c) -> p g c", c=NCMP), func=ACT.Gelu_apprx_tanh, bias=par("cmp_b1", i))
            for n, j, i in steps(act, 12):
                mod_row(1, n)
            for q in range(2):
                act.wait_ge(dve_tile_ready, tiles.next())
                go(s_p[:, q, 0:HEADS * NCMP], s_p[:, q, 0:HEADS * NCMP], ACT.Exp).then_inc(act_tile_ready, 1)
            softmax("nsa", 0)
            ffn(1, "nsa_out")
            norm(S, after("ffn_out1"))

            def dual_norm(N, ready, l, shift):
                norm(N, ready)
                for k in range(KD):
                    for s in range(N // S):
                        act.wait_ge(scaled_ready, scaled.next())
                        hh = h[:, k, s * S:(s + 1) * S]
                        go(hh, hh, ACT.Identity, bias=mods[:, l, shift + k, s:s + 1]).then_inc(h_ready, 1)

            def dual(l):
                N = S2 if l == 0 else S
                if l == 0:
                    act.wait_ge(ctx_landed, 16)
                    dual_norm(S2, lambda k: act.wait_ge(first_done, k + 1), l, 0)
                else:
                    dual_norm(S2, after("mlp_out0"), l, 0)
                for n in range(2):
                    for e in range(2):
                        act.wait_ge(acc_free[e], USED[f"conv_in{l}"][e] + n)
                        copy(f"conv_in{l}", 2 + e, n, s_p[:, e, 0:N], acc[2 + e][:, 0:N], func=ACT.Sigmoid)
                for m in range(4):
                    copy(f"naq{l}", m, 0, a_naq[:, m, 0:N], acc[m][:, 0:N], scale=DH ** -0.5)
                for m in range(4):
                    copy(f"nak{l}", m, 0, a_nak[:, m, :], acc[m][:])
                for m in range(4):
                    copy(f"nav{l}", m, 0, a_nav[:, m, :], acc[m][:])
                for m in range(4):
                    copy(f"gq{l}", m, 0, a_gq[:, m, 0:N], acc[m][:, 0:N])
                for m in range(2):
                    copy(f"gkv{l}", m, 0, a_gk[:, m, :], acc[m][:])
                for m in range(2):
                    copy(f"gkv{l}", 2 + m, 0, a_gv[:, 2 * m:2 * m + 2, :].rearrange("p a b -> p (a b)"), acc[2 + m][:, 0:2 * P])
                freed(f"gkv{l}", 3, 0)
                act.wait_ge(conv_done, KC * (l + 1))
                for c in range(6):
                    n = N if c < 4 else S2
                    src = a_gq[:, c, :] if c < 4 else a_gk[:, c - 4, :]
                    if c:
                        act.wait_ge(rotated, rot.next())
                    go(s_p[:, 0, 0:n], src[:, 0:n], ACT.Square).then_inc(act_operand_ready, 1)
                    root_of(n, scale=1.0 / DH if c < 4 else 1.0)
                act.wait_ge(rotated, rot.next())
                for c in range(KC):
                    act.wait_ge(centred, cen.next())
                    if c >= 2:
                        act.wait_ge(ln_summed, KC * l + c - 1)
                    go(s_p[:, c % 2, 0:N], a_cy[:, c, 0:N], ACT.Square).then_inc(act_operand_ready, 1)
                root_of(N)
                for c in range(KC):
                    act.wait_ge(centred, cen.next())
                    go(a_cy[:, c, 0:N], a_cy[:, c, 0:N], ACT.Silu, scale=par("ln_g", l * KC + c),
                       bias=par("ln_b", l * KC + c)).then_inc(act_operand_ready, 1)
                softmax("gqa", l)
                softmax("na", l)
                for br in range(3):
                    for n in range(2):
                        for m in range(4):
                            copy(f"gates{l}{br}", m, n, a_sig[:, 4 * n + m, 0:N], acc[m][:, 0:N], func=ACT.Sigmoid)
                dual_norm(N, after(f"out{l}"), l, 24)
                st = f"mlp_in{l}"
                for n, j, i in steps(act, 11):
                    for e in range(2):
                        act.wait_ge(acc_free[2 + e], n + USED[st][2 + e])
                        copy(st, e, n, m_silu[:, e, 0:N], acc[e][:, 0:N], func=ACT.Silu)

            for l in range(DEPTH):
                dual(l)
            norm(S, after("mlp_out1"))

        @block.vector
        def _(dve):
            V = nc.vector
            step, roots, at, sums, aux, turn_c, jobs_done = (Count() for _ in range(7))

            def link(ins):
                ins.then_inc(dve_step, 1)
                dve.wait_ge(dve_step, step.next())

            def full(stage, b, n):
                dve.wait_ge(acc_full[b], n + (USED[stage][b] + 1))

            def inverse(bank, N, width):
                link(V.tensor_scalar(rs[:, 0:N], bank[:, 0:N], 1.0 / width, EPS, ALU.mult, ALU.add))
                V.reciprocal(rs[:, 0:N], rs[:, 0:N]).then_inc(inverse_ready, 1)
                dve.wait_ge(root_ready, roots.next())

            def norm(N, gain, to, signal):
                dve.wait_ge(sums_ready, sums.next())
                inverse(psO, N, D)
                for k in range(KD):
                    V.scalar_tensor_tensor(out=to[:, k, 0:N], in0=x[:, k, 0:N], scalar=gain(k), in1=rs[:, 0:N],
                                           op0=ALU.mult, op1=ALU.mult).then_inc(signal, 1)

            def mod_take(l, n):
                dve.wait_ge(mod_turned, turn_c.next())
                b = prm[:, bass.ds(n * 4 + (PARAM["b_mod"] + 48 * l), 4)]
                V.tensor_tensor(mods[:, l, bass.ds(n * 4, 4), :], psT[:].rearrange("p (a s) -> p a s", s=P)[:, :, 0:2],
                                b.unsqueeze(2).broadcast_to([P, 4, 2]), ALU.add).then_inc(mod_taken, 1)

            def residual(stage):
                for m in range(KD):
                    full(stage, m % 4, m // 4)
                    V.tensor_tensor(x[:, m, 0:S], x[:, m, 0:S], acc[m % 4][:, 0:S], ALU.add).then_inc(acc_free[m % 4], 1)

            dve.wait_ge(params_landed, 32)
            a_, e_, z_, z2_, s_ = par("a_param", 0, KL), sca[:, 0:10], sca[:, 10:20], sca[:, 20:30], sca[:, 30:40]
            link(V.tensor_scalar(e_, a_, -1.0, None, ALU.mult))
            V.tensor_tensor(e_, e_, a_, ALU.min).then_inc(dve_tile_ready, 1)
            norm(S, lambda k: par("lru_g", k), h, h_ready)
            dve.wait_ge(act_tile_ready, at.next())
            link(V.tensor_scalar(z2_, e_, 2.0, None, ALU.add))
            link(V.reciprocal(z2_, z2_))
            link(V.tensor_tensor(z_, e_, z2_, ALU.mult))
            link(V.tensor_tensor(z2_, z_, z_, ALU.mult))
            link(V.tensor_scalar(s_, z2_, 1.0 / 15, 1.0 / 13, ALU.mult, ALU.add))
            for d in (11, 9, 7, 5, 3, 1):
                link(V.tensor_tensor(s_, s_, z2_, ALU.mult))
                link(V.tensor_scalar(s_, s_, 1.0 / d, None, ALU.add))
            link(V.tensor_tensor(s_, s_, z_, ALU.mult))
            link(V.tensor_scalar(e_, a_, -1.0, 0.0, ALU.mult, ALU.max))
            link(V.scalar_tensor_tensor(out=e_, in0=s_, scalar=2.0, in1=e_, op0=ALU.mult, op1=ALU.add))
            link(V.tensor_scalar(sca[:, 20:30], e_, -8.0, None, ALU.mult))
            V.tensor_scalar(sca[:, 30:40], e_, 8.0, None, ALU.mult).then_inc(decay_ready, 1)
            for n in range(5):
                for e in range(2):
                    t = 2 * n + e
                    full("lru_in", 2 + e, n)
                    o, i = l_x[:, t, :], acc[2 + e][:, 0:S]
                    link(V.tensor_scalar(o, i, par("lru_cw", t * CONV_L + CONV_L - 1), par("lru_cb", t), ALU.mult, ALU.add))
                    for d in range(1, CONV_L):
                        ins = V.scalar_tensor_tensor(out=o[:, d:], in0=i[:, 0:S - d], scalar=par("lru_cw", t * CONV_L + CONV_L - 1 - d),
                                                     in1=o[:, d:], op0=ALU.mult, op1=ALU.add)
                        if d < CONV_L - 1:
                            link(ins)
                        else:
                            ins.then_inc(acc_free[2 + e], 1)
            for n in range(KL):
                dve.wait_ge(act_tile_ready, at.next())
                link(V.tensor_scalar(l_r[:, n, :], l_t[:, n, :], 1.0, None, ALU.add))
                link(V.reciprocal(l_r[:, n, :], l_r[:, n, :]))
                V.tensor_tensor(l_t[:, n, :], l_t[:, n, :], l_r[:, n, :], ALU.mult).then_inc(dve_tile_ready, 1)
                if n % 3 == 2:
                    mod_take(0, n // 3)
            for n in range(KL):
                dve.wait_ge(act_tile_ready, at.next())
                link(V.tensor_tensor(l_i[:, n, :], l_i[:, n, :], l_t[:, n, :], ALU.mult))
                link(V.tensor_tensor(l_i[:, n, :], l_i[:, n, :], l_x[:, n, :], ALU.mult))
                link(V.tensor_tensor_scan(l_r[:, n, :], l_b[:, n, :], l_i[:, n, :], 0.0, ALU.mult, ALU.add))
                V.tensor_tensor(l_y[:, n, :], l_y[:, n, :], l_r[:, n, :], ALU.mult).then_inc(operand_ready, 1)
                if n < 9:
                    mod_take(0, 3 + n)
            residual("lru_out")

            def ffn(l):
                norm(S, lambda k: par("ffn_g", l * KD + k), h, h_ready)
                st = f"ffn_in{l}"

                def column(name, n, per, i):
                    return prm[:, bass.ds(n * per + (PARAM[name] + i), 1)]

                for n, j, i in steps(dve, 12, (step, 2 * CONV_F - 2), (at, 2)):
                    for e in range(2):
                        full(st, e, n)
                        o, a = f_conv[:, e, :], acc[e][:, 0:S]
                        w = [column("ffn_cw", n, 2 * CONV_F, (l * KF1 + e) * CONV_F + d) for d in range(CONV_F)]
                        link(V.tensor_scalar(o, a, w[CONV_F - 1], column("ffn_cb", n, 2, l * KF1 + e), ALU.mult, ALU.add))
                        for d in range(1, CONV_F):
                            ins = V.scalar_tensor_tensor(out=o[:, d:], in0=a[:, 0:S - d], scalar=w[CONV_F - 1 - d], in1=o[:, d:],
                                                         op0=ALU.mult, op1=ALU.add)
                            if d < CONV_F - 1:
                                link(ins)
                            else:
                                ins.then_inc(acc_free[e], 1)
                    for e in range(2):
                        full(st, 2 + e, n)
                        dve.wait_ge(act_tile_ready, at.next())
                        o = f_hid[:, bass.ds(n * 2 + e, 1), :].rearrange("p a b -> p (a b)")
                        V.tensor_tensor(o, f_gelu[:, e, :], acc[2 + e][:, 0:S], ALU.mult).then_inc(acc_free[2 + e], 1)
                residual(f"ffn_out{l}")

            def softmax(kind, layer):
                jobs = attention_jobs(kind, layer)
                base = jobs_done.base
                parts = 2 if kind == "nsa" else 1
                for j in range(len(jobs) + 1):
                    if j < len(jobs):
                        t, p, q = jobs[j]
                        head = 2 * t + p
                        nk = len(key_blocks(kind, q)) * P
                        sc = psS[j % 2]
                        dve.wait_ge(score_full, base + j + 1)
                        v = sc[:, 0:parts * nk].rearrange("p (b k) -> p b k", b=parts)
                        if kind == "nsa":
                            slope = float(np.float32(2.0 ** (-8.0 * (head + 1) / HEADS)))
                            c = con("causal", q * S, nk).unsqueeze(1).broadcast_to([P, 2, nk])
                            link(V.scalar_tensor_tensor(out=v, in0=c, scalar=slope, in1=v, op0=ALU.mult, op1=ALU.add))
                        if kind == "na" and q < 2:
                            bias = a_rpb[:, head * 6 + 2 - 2 * q:head * 6 + 6 - 2 * q, :].rearrange("p a b -> p (a b)")
                            link(V.tensor_tensor(sc[:, 0:S], sc[:, 0:S], bias, ALU.add))
                        i = (j % 2) * 2
                        V.tensor_reduce(s_max[:, i:i + parts], v, AX, ALU.max, negate=True).then_inc(score_max, 1)
                    if j >= 1:
                        t, p, q = jobs[j - 1]
                        head = 2 * t + p
                        nk = len(key_blocks(kind, q)) * P
                        i = ((j - 1) % 2) * 2
                        dve.wait_ge(prob_exp, base + j)
                        link(V.reciprocal(s_rec[:, i:i + parts], s_sum[:, i:i + parts]))
                        if kind == "nsa":
                            g = n_gate[:, q, HEADS + head:2 * HEADS + head + 1:HEADS]
                            link(V.tensor_tensor(s_rec[:, i:i + 2], s_rec[:, i:i + 2], g, ALU.mult))
                        for br in range(parts):
                            o = s_p[:, (j - 1) % 2, br * nk:(br + 1) * nk]
                            ins = V.tensor_scalar(o, o, s_rec[:, i + br:i + br + 1], None, ALU.mult)
                        ins.then_inc(prob_ready, 1)
                jobs_done.base += len(jobs)

            ffn(0)
            norm(S, lambda k: par("nsa_g", k), h, h_ready)
            link(V.memset(n_hid, 0.0))
            link(V.memset(n_pc, 0.0))
            V.memset(n_vz, 0.0).then_inc(pads_ready, 1)
            for n in range(2):
                for g in range(KV):
                    full("nsa_kv", g, n)
                    V.tensor_copy(n_kc[0:DH, n, g, :], acc[g][0:DH, 0:S])
                    V.tensor_copy(n_kc[DH:P, n, g, 0:S - 1], acc[g][DH:P, 1:S]).then_inc(acc_free[g], 1)
            for kv in range(2):
                dve.wait_ge(acc_free[3], USED["nsa_kv"][3] + kv + 1)
                for jj in range(HALF):
                    o = n_blk[:, kv * HALF + jj, :].rearrange("p (g c) -> p g c", c=NCMP)
                    i = n_kc[:, kv, :, 2 * jj:2 * jj + CMP_STRIDE * (NCMP - 1) + 1:CMP_STRIDE]
                    ins = V.tensor_scalar(o, i, par("cmp_pos", kv * HALF + jj), None, ALU.add)
                ins.then_inc(operand_ready, 1)
            for m in range(2):
                dve.wait_ge(acc_free[2 + m], USED["cmp"][2 + m] + 1)
                for g in range(KV):
                    ins = V.tensor_copy(n_hv[:, m * KV + g, :].rearrange("p (r c) -> p r c", c=CMPW),
                                        n_hid[:, 2 + m, g * CMPW:(g + 1) * CMPW].unsqueeze(1).broadcast_to([P, 4, CMPW]))
            ins.then_inc(operand_ready, 1)
            for n, j, i in steps(dve, 12, (turn_c, 1)):
                mod_take(1, n)
            full("cmp2", 0, 0)
            V.tensor_copy(n_ck[:, 0, :], acc[0][:, 0:KV * NCMP]).then_inc(acc_free[0], 1)
            full("cmp2", 1, 0)
            dve.wait_ge(pads_ready, 1)
            vz = n_vz.rearrange("p (g r) d -> p g r d", r=GROUP)
            for r in range(GROUP):
                rows_ = slice(r * CMPW, (r + 1) * CMPW)
                ins = V.tensor_copy(vz[rows_, :, r, :], acc[1][rows_, 0:KV * DH].rearrange("p (g d) -> p g d", d=DH))
            ins.then_inc(acc_free[1], 1)
            W = HEADS * NCMP
            for q in range(2):
                sc = s_p[:, q, 0:W]
                sc3 = sc.rearrange("p (h c) -> p h c", c=NCMP)
                dve.wait_ge(pe_aux_full, aux.next())
                for p in range(2):
                    by_half = [v.rearrange("p (t e c) -> p t e c", e=2, c=NCMP)[:, :, p, :] for v in (sc, con("cmp_bias", q * W, W))]
                    ins = V.tensor_tensor(by_half[0], cmp_banks[q][p][:, 0:W // 2].rearrange("p (t c) -> p t c", c=NCMP), by_half[1], ALU.add)
                link(ins)
                link(V.tensor_reduce(s_cm, sc3, AX, ALU.max))
                V.tensor_tensor(sc3, sc3, s_cm.unsqueeze(2).broadcast_to([P, HEADS, NCMP]), ALU.subtract).then_inc(dve_tile_ready, 1)
                dve.wait_ge(act_tile_ready, at.next())
                link(V.reduce_sum(s_cs, sc3, AX))
                link(V.reciprocal(s_cr, s_cs))
                link(V.tensor_tensor(s_cr, s_cr, n_gate[:, q, 0:HEADS], ALU.mult))
                link(V.tensor_tensor(sc3, sc3, s_cr.unsqueeze(2).broadcast_to([P, HEADS, NCMP]), ALU.mult))
                V.tensor_tensor(n_pc[:, q, :].rearrange("p (h c) -> p h c", c=CMPW)[:, :, 0:NCMP], sc3,
                                con("cmp_mask", q * NCMP, NCMP).unsqueeze(1).broadcast_to([P, HEADS, NCMP]), ALU.mult).then_inc(operand_ready, 1)
                dve.wait_ge(operand_ready, KL + 3 + q + 1)
            for q in range(2):
                dve.wait_ge(pe_aux_full, aux.next())
                V.tensor_copy(n_pcT[:, q, :, :].rearrange("p g k -> p (g k)"), (psT, psO)[q][:]).then_inc(pe_aux_free, 1)
            softmax("nsa", 0)
            residual("nsa_out")
            ffn(1)
            norm(S, lambda k: par("final_g", k), x, first_done)

            def dual_residual(stage, l, gate, N):
                for m in range(KD):
                    full(stage, m % 4, m // 4)
                    for s in range(N // S):
                        o = x[:, m, s * S:(s + 1) * S]
                        ins = V.scalar_tensor_tensor(out=o, in0=acc[m % 4][:, s * S:(s + 1) * S], scalar=mods[:, l, gate + m, s:s + 1], in1=o,
                                                     op0=ALU.mult, op1=ALU.add)
                    ins.then_inc(acc_free[m % 4], 1)

            def dual_norm(N, which):
                dve.wait_ge(sums_ready, sums.next())
                inverse(psO, N, D)
                for k in range(KD):
                    for s in range(N // S):
                        c = slice(s * S, (s + 1) * S)
                        V.scalar_tensor_tensor(out=h[:, k, c], in0=x[:, k, c], scalar=gn[:, which, s, k:k + 1], in1=rs[:, c],
                                               op0=ALU.mult, op1=ALU.mult).then_inc(scaled_ready, 1)

            def dual(l):
                N = S2 if l == 0 else S
                ns = N // S
                for which in range(2):
                    for s in range(2):
                        link(V.scalar_tensor_tensor(out=gn[:, which, s, :], in0=mods[:, l, 24 * which + 8:24 * which + 16, s], scalar=1.0,
                                                    in1=par(f"norm{which + 1}", l * KD, KD), op0=ALU.add, op1=ALU.mult))
                dual_norm(S2, 0)
                link(V.memset(a_u[:, :, 0:HALO], 0.0))
                V.memset(a_u[:, :, HALO + S:], 0.0).then_inc(rpb_place, 1)
                for n in range(2):
                    for e in range(2):
                        full(f"conv_in{l}", e, n)
                        dve.wait_ge(acc_free[2 + e], USED[f"conv_in{l}"][2 + e] + n + 1)
                        V.tensor_tensor(a_u3[:, 2 * n + e, 0:ns, HALO:HALO + S], acc[e][:, 0:N].rearrange("p (s t) -> p s t", t=S),
                                        s_p[:, e, 0:N].rearrange("p (s t) -> p s t", t=S), ALU.mult).then_inc(acc_free[e], 1)
                for e in range(2):
                    dve.wait_ge(acc_free[e], USED[f"conv_in{l}"][e] + 2)
                cy = a_cy.rearrange("p c (s t) -> p c s t", t=S)

                def conv(c, j):
                    w = prm[:, bass.ds(j + (PARAM["conv_w"] + (l * KC + c) * CONV_K), 1)]
                    return V.scalar_tensor_tensor(out=cy[:, c, 0:ns, :], in0=a_u3[:, c, 0:ns, bass.ds(j, S)], scalar=w, in1=cy[:, c, 0:ns, :],
                                                  op0=ALU.mult, op1=ALU.add)

                for c in range(KC):
                    V.tensor_scalar(cy[:, c, 0:ns, :], a_u3[:, c, 0:ns, 0:S], par("conv_w", (l * KC + c) * CONV_K), par("conv_b", l * KC + c),
                                    ALU.mult, ALU.add).then_inc(dve_step, 1)
                with dve.Fori(1, CONV_K - 1) as j:
                    for c in range(KC):
                        dve.wait_ge(dve_step, j * KC + (step.base + c - KC + 1))
                        conv(c, j).then_inc(dve_step, 1)
                step.base += (CONV_K - 1) * KC
                dve.wait_ge(dve_step, step.base)
                for c in range(KC):
                    conv(c, CONV_K - 1).then_inc(conv_done, 1)
                dve.wait_ge(conv_done, KC * (l + 1))
                for c in range(6):
                    n = N if c < 4 else S2
                    src = a_gq[:, c, :] if c < 4 else a_gk[:, c - 4, :]
                    dve.wait_ge(pe_aux_full, aux.next())
                    inverse(psS[0], n, DH)
                    V.scalar_tensor_tensor(out=src[:, 0:n], in0=src[:, 0:n], scalar=par("q_g" if c < 4 else "k_g", l), in1=rs[:, 0:n],
                                           op0=ALU.mult, op1=ALU.mult).then_inc(operand_ready, 1)
                    dve.wait_ge(pe_aux_full, aux.next())
                    link(V.tensor_tensor(s_p[:, 1, 0:S], psS[1][:, 0:S], con("sin", 0, S), ALU.mult))
                    link(V.tensor_tensor(src[:, 0:S], src[:, 0:S], con("cos", 0, S), ALU.mult))
                    V.tensor_tensor(src[:, 0:S], src[:, 0:S], s_p[:, 1, 0:S], ALU.add).then_inc(rotated, 1)
                dve.wait_ge(pe_aux_full, aux.next())
                link(V.tensor_scalar(rs[:, 0:N], psT[:, 0:N], 1.0 / CW, None, ALU.mult))
                for c in range(KC):
                    V.tensor_tensor(a_cy[:, c, 0:N], a_cy[:, c, 0:N], rs[:, 0:N], ALU.subtract).then_inc(centred, 1)
                dve.wait_ge(ln_summed, KC * (l + 1))
                inverse(psO, N, CW)
                for c in range(KC):
                    V.tensor_tensor(a_cy[:, c, 0:N], a_cy[:, c, 0:N], rs[:, 0:N], ALU.mult).then_inc(centred, 1)
                softmax("gqa", l)
                dve.wait_ge(rpb_ready, l + 1)
                softmax("na", l)
                for br in range(3):
                    st = f"branch{l}{br}"
                    for m in range(KD):
                        full(st, m % 4, m // 4)
                        if m < 4:
                            dve.wait_ge(acc_free[m], USED[f"gates{l}{br}"][m] + 2)
                        o, g, a = a_y[:, m, 0:N], a_sig[:, m, 0:N], acc[m % 4][:, 0:N]
                        if br == 0:
                            V.tensor_tensor(o, a, g, ALU.mult).then_inc(acc_free[m % 4], 1)
                        else:
                            link(V.tensor_tensor(s_p[:, m % 2, 0:N], a, g, ALU.mult))
                            V.tensor_tensor(o, o, s_p[:, m % 2, 0:N], ALU.add).then_inc(acc_free[m % 4], 1)
                dual_residual(f"out{l}", l, 16, N)
                dual_norm(N, 1)
                st = f"mlp_in{l}"
                for n, j, i in steps(dve, 11):
                    for e in range(2):
                        full(st, 2 + e, n)
                        dve.wait_ge(acc_free[e], n + (USED[st][e] + 1))
                        o = m_hid[:, bass.ds(n * 2 + e, 1), :].rearrange("p a b -> p (a b)")[:, 0:N]
                        V.tensor_tensor(o, m_silu[:, e, 0:N], acc[2 + e][:, 0:N], ALU.mult).then_inc(acc_free[2 + e], 1)
                dual_residual(f"mlp_out{l}", l, 40, N)

            for l in range(DEPTH):
                dual(l)
            norm(S, lambda k: par("final2", k), h, out_ready)


def constants():
    c = np.zeros((P, CONST["end"]), np.float32)

    def put(name, a):
        a = a.reshape(P, -1)
        c[:, CONST[name]:CONST[name] + a.shape[1]] = a

    put("ident", np.eye(P))
    put("ones", np.ones((P, P)))
    p = np.arange(P)
    put("heads1", (p[:, None] // DH == p[None, :] // DH).astype(np.float32))
    r = np.zeros((P, P))
    for i in range(P):
        if i % 32 < 16:
            r[i + 16, i] = -1.0
        else:
            r[i - 16, i] = 1.0
    put("rope", r)
    half = DH // 2
    freqs = np.power(np.float32(10000.0), -np.arange(0, half, 2, dtype=np.float32) / half).astype(np.float32)
    t = np.arange(S)
    ang = np.zeros((P, S), np.float32)
    for i in range(P):
        ang[i] = (t // GRID if i % DH < half else t % GRID).astype(np.float32) * freqs[i % 16]
    put("cos", np.cos(ang))
    put("sin", np.sin(ang))
    q = np.arange(S).reshape(2, P)
    dist = q[:, :, None] - np.arange(S)[None, None, :]
    put("causal", np.where(dist >= 0, -dist, NEG).transpose(1, 0, 2))
    start = np.arange(NCMP) * CMP_STRIDE
    end, centre = start + CMP_BLOCK - 1, start + (CMP_BLOCK - 1) / 2.0
    slopes = (2.0 ** (-8.0 * np.arange(1, HEADS + 1) / HEADS)).astype(np.float32)
    ok = end[None, None, :] <= q[:, :, None]
    d = (q[:, :, None] - centre[None, None, :]).astype(np.float32)
    b = np.where(ok[:, :, None, :], -slopes[None, None, :, None] * d[:, :, None, :], NEG)
    put("cmp_bias", b.transpose(1, 0, 2, 3))
    put("cmp_mask", ok.astype(np.float32).transpose(1, 0, 2))
    win0 = np.clip(p % GRID - 8, 0, GRID - 16)[:, None]
    kc = np.arange(GRID)[None, :]
    put("na_mask", np.where((kc >= win0) & (kc < win0 + 16), 0.0, NEG))
    return c


def tiles_of(w):
    k, m = w.shape
    return w.reshape(k // P, P, m // P, P).transpose(2, 0, 1, 3).reshape(-1, P, P)


def rows_of(w):
    k, m = w.shape
    return w.reshape(k // P, P, m // P, P).transpose(0, 2, 1, 3).reshape(-1, P, P)


def twice(w):
    k, m = w.shape
    w = w.reshape(k, m // DH, 1, DH)
    return np.concatenate([w, w], axis=2).reshape(k, 2 * m)


def pairs(w, half, width=2 * P):
    return [tiles_of(np.concatenate([w[:, i:i + width], w[:, half + i:half + i + width]], axis=1)) for i in range(0, half, width)]


def weight_stream(a):
    out = np.zeros((UNITS, P, TILES, P), np.float32)
    units = {s[0]: s[1] for s in STREAM}

    def put(name, *parts):
        dst, t = out[FIRST_UNIT[name]:FIRST_UNIT[name] + units[name]], 0
        for part in parts:
            for tile in part:
                dst[t // TILES, :, t % TILES, :] = tile
                t += 1
        assert units[name] - 1 < t / TILES <= units[name], (name, t)

    put("lru_in", *pairs(a["lru_w_in"][0], LRU))
    put("lru_gate", a["lru_gate_w"][0].transpose(1, 0, 2, 3).reshape(2 * KL, P, P))
    put("lru_out", tiles_of(a["lru_w_out"][0]))
    for l in range(DEPTH):
        put(f"mod{l}", *[rows_of(a["w_mod_2"][l][:, i:i + 512]) for i in range(0, 6 * D, 512)])
        put(f"ffn_in{l}", *pairs(a["ffn_w_in"][l], FF1))
        put(f"ffn_out{l}", tiles_of(a["ffn_w_out"][l]))
    w = a["nsa_w_in"][0]
    put("nsa_q", tiles_of(w[:, 0:D]))
    kv = w[:, D:D + 1536].reshape(D, 3, 2, KV * DH)
    put("nsa_kv", *[tiles_of(twice(kv[:, b, c])) for b, c in ((0, 0), (0, 1), (1, 0), (2, 0))])
    put("nsa_v", rows_of(np.concatenate([kv[:, 1, 1], kv[:, 2, 1]], axis=1)))
    g = np.zeros((D, P), np.float32)
    g[:, 0:48] = w[:, D + 1536:]
    put("nsa_gate", rows_of(g))
    put("cmp", *[tiles_of(a["nsa_cmp_w1"][0, i]) for i in range(2)])
    put("nsa_out", tiles_of(a["nsa_w_out"][0]))
    for l in range(DEPTH):
        w = a["w_in_2"][l]
        o = np.cumsum([0, 1024, 512, 512, 512, 512, 128, 128, 3072])
        put(f"in{l}", *pairs(w[:, 0:1024], 512), tiles_of(w[:, o[1]:o[2]]), tiles_of(w[:, o[2]:o[3]]), rows_of(w[:, o[3]:o[4]]),
            tiles_of(w[:, o[4]:o[5]]))
        put(f"in_gkv{l}", tiles_of(twice(w[:, o[5]:o[6]])), rows_of(w[:, o[6]:o[7]]))
        for b, name in enumerate(("w_conv_out_2", "w_na_out_2", "w_gqa_out_2")):
            put(f"gates{l}{b}", tiles_of(w[:, o[7] + b * D:o[7] + (b + 1) * D]))
            put(f"branch{l}{b}", tiles_of(a[name][l]))
        put(f"out{l}", tiles_of(a["w_out_2"][l]))
        put(f"mlp_in{l}", *pairs(a["w_ffn_in_2"][l], FF2))
        put(f"mlp_out{l}", tiles_of(a["w_ffn_out_2"][l]))
    return out.reshape(UNITS, P, TILES * P)


def parameters(a):
    out = np.zeros((P, PARAM["end"]), np.float32)

    def put(name, v):
        v = v.reshape(P, -1)
        out[:, PARAM[name]:PARAM[name] + v.shape[1]] = v

    def col(v):
        n = v.shape[-1] // P
        return np.moveaxis(v.reshape(v.shape[:-1] + (n, P)), -1, 0)

    def taps(w):
        l, k, c = w.shape
        return w.reshape(l, k, c // P, P).transpose(3, 0, 2, 1)

    for name, key in (("lru_g", "lru_norm_g"), ("nsa_g", "nsa_norm_g"), ("ffn_g", "ffn_norm_g"), ("final_g", "final_norm_g"),
                      ("norm1", "norm1_g_2"), ("norm2", "norm2_g_2"), ("final2", "final_g_2"), ("lru_cb", "lru_conv_b"),
                      ("gate_b", "lru_gate_b"), ("a_param", "lru_a_param"), ("ffn_cb", "ffn_conv_b"), ("cmp_b1", "nsa_cmp_b1"),
                      ("b_mod", "b_mod_2"), ("conv_b", "conv_b_2"), ("ln_g", "conv_ln_g_2"), ("ln_b", "conv_ln_b_2")):
        put(name, col(a[key]))
    for name, key in (("lru_cw", "lru_conv_w"), ("ffn_cw", "ffn_conv_w"), ("conv_w", "conv_w_2")):
        put(name, taps(a[key]))
    put("cmp_pos", a["nsa_cmp_pos"][0].reshape(2, HALF, P).transpose(2, 0, 1))
    for name, key in (("q_g", "q_norm_g_2"), ("k_g", "k_norm_g_2")):
        put(name, np.concatenate([a[key].T, a[key].T], axis=0))
    put("c", np.stack([a["c_2"][0].reshape(KD, P).T, a["c_ctx_2"].reshape(KD, P).T], axis=2))
    w2 = a["nsa_cmp_w2"][0].reshape(2, 2, P, DH)
    put("w2k", np.concatenate([w2[0], w2[0]], axis=2).transpose(1, 0, 2))
    put("w2v", w2[1].transpose(1, 0, 2))
    return out


def position_biases(rpb):
    r, qc = np.arange(P) // GRID, np.arange(P) % GRID
    rows = 4 + np.arange(6)[None, :] + (1 - r)[:, None]
    cols = np.clip(np.arange(GRID)[None, :] - qc[:, None] + 15, 0, 30)
    b = rpb[:, :, rows[:, :, None], cols[:, None, :]]
    return np.ascontiguousarray(b.transpose(0, 2, 1, 3, 4)).reshape(rpb.shape[0], P, -1)


def layout(inputs):
    a = {k: np.asarray(v) for k, v in inputs.items()}
    both = np.concatenate([a["x"][0].T.reshape(KD, P, S), a["ctx_2"][0].T.reshape(KD, P, S)], axis=2)
    return {"wstream": weight_stream(a), "params": parameters(a), "consts": constants(),
            "rpb": position_biases(a["na_rpb_2"]), "x_in": np.ascontiguousarray(both.transpose(1, 0, 2))}


SHAPES = {"wstream": (UNITS, P, TILES * P), "params": (P, PARAM["end"]), "consts": (P, CONST["end"]),
          "rpb": (DEPTH, P, 48 * GRID), "x_in": (P, KD, S2)}


def kernel(**inputs):
    import concourse.bacc as bacc
    from concourse.bass_utils import run_bass_kernel_spmd

    nc = bacc.Bacc("TRN2", target_bir_lowering=False, num_devices=1)
    aps = [nc.dram_tensor(n, s, F32, kind="ExternalInput").ap() for n, s in SHAPES.items()]
    out = nc.dram_tensor("out", (P, KD, S), F32, kind="ExternalOutput").ap()
    program(nc, *aps, out)
    r = run_bass_kernel_spmd(nc, [layout(inputs)], core_ids=[0])
    out = r.results[0]["out"]
    return np.ascontiguousarray(out.transpose(2, 1, 0)).reshape(1, S, D)
```

```python
import numpy as np

import concourse.bass as bass
from concourse import mybir
from contextlib import ExitStack

F32 = mybir.dt.float32
F32R = mybir.dt.float32r
ALU = mybir.AluOpType
ACT = mybir.ActivationFunctionType
AX = mybir.AxisListType.X

P = 128
D = 1024
KD = D // P
S = 256
S2 = 2 * S
EPS = 1e-6
LRU = 1280
KL = LRU // P
CONV_L = 4
FF1 = 3072
KF1 = FF1 // P
CONV_F = 3
HEADS = 16
DH = 64
KV = 4
GROUP = HEADS // KV
CMP_BLOCK, CMP_STRIDE = 32, 16
NCMP = (S - CMP_BLOCK) // CMP_STRIDE + 1
CMPW = 32
HID = 256
CW = 512
KC = CW // P
CONV_K = 31
HALO = CONV_K // 2
FF2 = 2816
KF2 = FF2 // P
GRID = 64
NEG = -1e30

TILES = 32
HALF = TILES // 2
SLOTS = 4
JOB = 8
SPLITS = 4
AHEAD = SPLITS - 1
BODIES = 2
HALF_A, HALF_B = 6, 5
DEPTH = 2


def columns(parts):
    at, where = 0, {}
    for name, n in parts:
        where[name] = at
        at += n
    where["end"] = at
    return where


PARAM = columns([
    ("lru_g", KD), ("nsa_g", KD), ("ffn_g", 2 * KD), ("final_g", KD), ("norm1", 2 * KD), ("norm2", 2 * KD),
    ("final2", KD), ("lru_cw", KL * CONV_L), ("lru_cb", KL), ("gate_b", 2 * KL), ("a_param", KL),
    ("ffn_cw", 2 * KF1 * CONV_F), ("ffn_cb", 2 * KF1), ("cmp_b1", 4), ("cmp_pos", 2 * HALF),
    ("b_mod", 2 * 48), ("conv_w", 2 * KC * CONV_K), ("conv_b", 2 * KC), ("ln_g", 2 * KC), ("ln_b", 2 * KC),
    ("q_g", 2), ("k_g", 2), ("c", 2 * KD), ("w2k", 2 * P), ("w2v", 2 * DH),
])
CONST = columns([
    ("ident", P), ("head_sel", 22), ("rope", P), ("cos", S), ("sin", S), ("causal", 2 * S),
    ("cmp_bias", 2 * HEADS * NCMP), ("cmp_mask", 2 * NCMP), ("na_mask", GRID),
])

SPLIT, DIRECT, VECTOR = "split", "direct", "vector"
MOD_V = 3
STREAM = [("lru_in", 160, SPLIT), ("lru_gate", 20, DIRECT), ("mod0", TILES * (12 - MOD_V), DIRECT), ("lru_out", 80, DIRECT),
          ("ffn_in0", 384, SPLIT), ("ffn_out0", 192, SPLIT), ("nsa_q", 64, SPLIT), ("nsa_kv", 128, SPLIT),
          ("nsa_v", 32, SPLIT), ("nsa_gate", 8, SPLIT), ("mod0v", 32, VECTOR), ("cmp", 32, DIRECT), ("mod0v", 32, VECTOR), ("cmp", 32, DIRECT),
          ("mod0v", TILES * MOD_V - 64, VECTOR), ("nsa_out", 64, DIRECT),
          ("ffn_in1", 384, SPLIT), ("ffn_out1", 192, SPLIT)]
for _l in range(DEPTH):
    STREAM += [(f"in{_l}", 192, SPLIT), (f"in_gkv{_l}", 24, SPLIT)]
    for _b in range(3):
        if _l == 0:
            STREAM += [(f"gates{_l}{_b}", 32, SPLIT), ("mod1", 32, VECTOR), (f"gates{_l}{_b}", 32, SPLIT), ("mod1", 96, VECTOR)]
        else:
            STREAM += [(f"gates{_l}{_b}", 64, SPLIT)]
        STREAM += [(f"branch{_l}{_b}", 32, DIRECT)]
    STREAM += [(f"out{_l}", 64, SPLIT), (f"mlp_in{_l}a", TILES * HALF_A, SPLIT), (f"mlp_out{_l}a", 16 * HALF_A, SPLIT),
               (f"mlp_in{_l}b", TILES * HALF_B, SPLIT), (f"mlp_out{_l}b", 16 * HALF_B, SPLIT)]
STAGE_HALVES, FIRST_JOB = {}, {}
HALF_TILES, HALF_KIND, JOBS, RUN_LAST = [], [], [], []
_direct = True
for _name, _tiles, _kind in STREAM:
    FIRST_JOB.setdefault(_name, len(JOBS))
    if _kind == SPLIT and _direct:
        _start = len(JOBS)
    if _kind != VECTOR:
        _direct = _kind == DIRECT
    while _tiles > 0:
        if _kind == SPLIT:
            JOBS += [(len(HALF_TILES), i) for i in range(min(_tiles, HALF) // JOB)]
        STAGE_HALVES.setdefault(_name, []).append(len(HALF_TILES))
        HALF_TILES.append(min(_tiles, HALF))
        HALF_KIND.append(_kind)
        _tiles -= HALF
    if _kind == SPLIT:
        RUN_LAST = RUN_LAST[:_start] + [len(JOBS) - 1] * (len(JOBS) - _start)
HALVES = len(HALF_TILES)
FIRST_HALF = {n: v[0] for n, v in STAGE_HALVES.items()}
LAST_JOB = {v: j for j, (v, _) in enumerate(JOBS)}
PLACE = {v: HALF_KIND[:v].count(HALF_KIND[v]) for v in range(HALVES)}
DOTS = 8


BANKS = [("lru_in", (5, 5, 5, 5)), ("lru_gate", (3, 3, 2, 2)), ("mod0", (0, 0, 0, 12 - MOD_V)), ("lru_out", (2,) * 4),
         ("ffn_in0", (12,) * 4), ("ffn_out0", (2,) * 4), ("nsa_q", (2,) * 4), ("nsa_kv", (4,) * 4),
         ("nsa_v", (1, 1, 0, 0)), ("nsa_gate", (0, 0, 1, 1)), ("cmp", (1,) * 4),
         ("cmp2", (1, 1, 0, 0)), ("nsa_out", (2,) * 4), ("ffn_in1", (12,) * 4), ("ffn_out1", (2,) * 4)]
for _l in range(DEPTH):
    BANKS += [(f"conv_in{_l}", (2,) * 4), (f"naq{_l}", (1,) * 4), (f"nak{_l}", (1,) * 4), (f"nav{_l}", (1,) * 4),
              (f"gq{_l}", (1,) * 4), (f"gkv{_l}", (1,) * 4)]
    for _b in range(3):
        BANKS += [(f"gates{_l}{_b}", (2,) * 4), (f"branch{_l}{_b}", (2,) * 4)]
    BANKS += [(f"out{_l}", (2,) * 4), (f"mlp_in{_l}a", (HALF_A,) * 4), (f"mlp_out{_l}a", (2,) * 4),
              (f"mlp_in{_l}b", (HALF_B,) * 4), (f"mlp_out{_l}b", (2,) * 4)]
USED, _c = {}, [0, 0, 0, 0]
for _name, _uses in BANKS:
    USED[_name] = list(_c)
    _c = [a + b for a, b in zip(_c, _uses)]


HIDDEN, _c = {}, 0
for _name, _chunks in ([("ffn0", KF1), ("ffn1", KF1)] + [(f"mlp{_l}{_p}", _n) for _l in range(DEPTH) for _p, _n in (("a", 2 * HALF_A), ("b", 2 * HALF_B))]):
    HIDDEN[_name] = _c
    _c += _chunks


class Count:

    def __init__(self, base=0):
        self.base, self.k, self.per, self.n = base, 0, 0, None

    def next(self, k=1):
        if self.n is None:
            self.base += k
            return self.base
        self.k += k
        return self.n * self.per + (self.base + self.k)

    def enter(self, per):
        self.per = per

    def at(self, n):
        self.n, self.k = n, 0

    def leave(self, steps):
        assert self.k == self.per, (self.k, self.per)
        self.base += self.per * steps
        self.n = None


def steps(eng, count, *counts, peel=0):
    for c, per in counts:
        c.enter(per)
    turns = count // BODIES

    def body(n):
        for c, _ in counts:
            c.at(n)

    for n in range(peel * BODIES):
        body(n)
        yield n, n % BODIES, n // BODIES
    with eng.Fori(peel, turns) as i:
        for j in range(BODIES):
            n = i * BODIES + j
            body(n)
            yield n, j, i
    for j in range(count - turns * BODIES):
        n = turns * BODIES + j
        body(n)
        yield n, j, turns
    for c, _ in counts:
        c.leave(count)


def attention_jobs(layer=None):
    if layer is None:
        return [("nsa", t, p, q) for t in range(HEADS // 2) for p in range(2) for q in range(2)]
    tiles = (0, 2) if layer == 0 else (0,)
    return [(kind, t, p, q0 + q) for kind in ("gqa", "na") for t in range(4) for q0 in tiles for p in range(2) for q in range(2)]


def key_blocks(kind, q):
    if kind == "nsa":
        return list(range(q + 1))
    return [0, 1, 2, 3] if q < 2 else [2, 3]


ARENA = 19200


def turned_blocks(kind, q):
    if kind == "nsa":
        return [2 * br + b for br in range(2) for b in range(q + 1)]
    return list(range(len(key_blocks(kind, q))))


def used(v, kind, q):
    n = len(key_blocks(kind, q)) * P
    return v.rearrange("p (b k) -> p b k", b=2)[:, :, 0:n] if kind == "nsa" else v[:, 0:n].unsqueeze(1)


def program(nc, wstream, params_in, consts_in, rpb_in, c_in, x_in, out):
    ctx = ExitStack()
    with ctx:
        def sb(name, shape, kind=F32):
            return ctx.enter_context(nc.sbuf_tensor(name, shape, kind))

        def sem(name):
            return ctx.enter_context(nc.semaphore(name))

        ring = sb("ring", [P, SLOTS, HALF * P])
        w_hi = sb("w_hi", [P, SPLITS, JOB * P], F32R)
        w_lo = sb("w_lo", [P, SPLITS, JOB * P], F32R)
        x = sb("x", [P, KD, S2])
        h_hi = sb("h_hi", [P, KD, S2], F32R)
        h_lo = sb("h_lo", [P, KD, S2], F32R)
        prm = sb("prm", [P, PARAM["end"]])
        cst = sb("cst", [P, CONST["end"]])
        ones = sb("ones", [P, P])
        eps = sb("eps", [P, 1])
        rs = sb("rs", [P, S2])
        small = sb("small", [P, 320])
        mods = sb("mods", [P, 2, 48, 2])
        mod_parts = sb("mod_parts", [P, 48, 2, 2])
        mrow = sb("mrow", [P, 512])
        gn = sb("gn", [P, 2, 2, KD])
        with nc.sbuf_tensor("arena", [P, ARENA], F32) as arena:
            pass
        hid_hi = sb("hid_hi", [P, KF1 * S], F32R)
        hid_lo = sb("hid_lo", [P, KF1 * S], F32R)

        def part(at, *shape):
            n = int(np.prod(shape))
            assert at + n <= ARENA, at + n
            a = arena[:, at:at + n]
            if len(shape) == 2:
                a = a.rearrange("p (a b) -> p a b", b=shape[1])
            if len(shape) == 3:
                a = a.rearrange("p (a b c) -> p a b c", b=shape[1], c=shape[2])
            return a

        def par(name, i=0, n=1):
            return prm[:, PARAM[name] + i:PARAM[name] + i + n]

        def con(name, i, n):
            return cst[:, CONST[name] + i:CONST[name] + i + n]

        ident, rope = (con(n, 0, P) for n in ("ident", "rope"))

        l_y, l_x, l_r, l_i, l_b, l_t = (part(i * KL * S, KL, S) for i in range(6))
        hidden_end = 2 * KF1 * S
        f_conv, f_gelu, f_prod = (part(hidden_end + i * 2 * S, 2, S) for i in range(3))
        m_silu, m_prod = (part(hidden_end + i * 2 * S2, 2, S2) for i in range(2))
        f_out = part(0, KD, S)
        f_hidden = [v[:].rearrange("p (c t) -> p c t", t=S) for v in (hid_hi, hid_lo)]
        m_hidden = [v[:].rearrange("p (c t) -> p c t", t=S2) for v in (hid_hi, hid_lo)]
        n_q = part(0, KD, S)
        n_kc = part(2048, 2, KV, S)
        n_k = part(4096, 2, KV, S)
        n_v = part(6144, 2, 512)
        n_gate = part(7168, 2, 48)
        n_blk = part(7264, 32, KV * NCMP)
        n_hid = part(9184, 4, KV * CMPW)
        n_ck = part(9696, 1, KV * NCMP)
        n_cv = part(9760, KV, DH)
        n_vz = part(10016, HEADS, DH)
        n_pc = part(11040, 2, HEADS * CMPW)
        n_pcT = part(12064, 2, KV, P)
        n_c = (part(14112, D), part(15136, D))
        n_hv = part(13088, 2 * KV, P)
        a_u = part(0, 2 * KC, S + 2 * HALO)
        a_u3 = a_u.rearrange("p (c s) t -> p c s t", s=2)
        a_rpb = part(2304, 8 * 6, GRID)
        a_y = part(0, KD, S2)
        a_cy = part(5376, KC, S2)
        a_nak, a_nav, a_naq = (part(7424 + 2048 * i, 4, S2) for i in range(3))
        a_sig = part(7424, KD, S2)
        a_c = (part(4096, D), part(15616, D))
        a_gq = part(13568, 4, S2)
        a_gk = part(15616, 2, S2)
        a_gv = part(16640, 4, P)
        s_p = part(17152, 4, S2)
        n_pT = part(14112, 4, S2)
        a_pT = part(0, 4, S2)
        sq = part(17152, 4, S2)
        scaled = part(17152, 8, S)
        s_cm = small[:, 0:16]
        s_cs = small[:, 16:32]
        s_cr = small[:, 32:48]
        s_max = small[:, 48:56]
        s_sum = small[:, 56:64]
        s_rec = small[:, 64:72]
        sca = small[:, 92:132]
        silc = small[:, 132:148].rearrange("p (k s) -> p k s", s=2)

        ps = [ctx.enter_context(nc.psum_tensor(f"ps{i}", [P, 512], F32)) for i in range(8)]
        acc, psS, psT, psO = ps[0:4], ps[4:6], ps[6], ps[7]
        head_rows, head_factors, head_turns = ps[4], (ps[5], ps[6]), (ps[7], ps[4])
        score_banks, turn_banks, out_banks = (ps[4], ps[5], ps[3]), (ps[6], ps[2]), (ps[7], ps[1])
        cmp_banks = (psS, (psT, psO))

        landed = [sem(f"landed{s}") for s in range(SLOTS)]
        raw_used = sem("raw_used")
        weights_rounded, weights_ready, weights_used = (sem(n) for n in ("weights_rounded", "weights_ready", "weights_used"))
        pool_written = sem("pool_written")
        params_landed, x_landed, rpb_landed, ctx_landed = sem("params_landed"), sem("x_landed"), sem("rpb_landed"), sem("ctx_landed")
        acc_full = [sem(f"acc_full{b}") for b in range(4)]
        acc_free = [sem(f"acc_free{b}") for b in range(4)]
        squares_ready, sums_ready, root_ready = (sem(n) for n in ("squares_ready", "sums_ready", "root_ready"))
        h_rounded = sem("h_rounded")
        scaled_ready, h_ready = sem("scaled_ready"), sem("h_ready")
        act_tile_ready = sem("act_tile_ready")
        dve_tile_ready = sem("dve_tile_ready")
        silu_ready, mod_turned, mod_taken = sem("silu_ready"), sem("mod_turned"), sem("mod_taken")
        pe_aux_full, pe_aux_free = sem("pe_aux_full"), sem("pe_aux_free")
        operand_ready = sem("operand_ready")
        act_operand_ready = sem("act_operand_ready")
        score_full, score_max, prob_exp, prob_ready = (sem(n) for n in ("score_full", "score_max", "prob_exp", "prob_ready"))
        turned_full, turned_ready, o_full, o_free = (sem(n) for n in ("turned_full", "turned_ready", "o_full", "o_free"))
        dve_step, act_step, pool_step = sem("dve_step"), sem("act_step"), sem("pool_step")
        c_landed, c_ready, mod_summed = sem("c_landed"), sem("c_ready"), sem("mod_summed")
        rpb_ready, rpb_place = sem("rpb_ready"), sem("rpb_place")
        head_summed, head_spread, head_turned = sem("head_summed"), sem("head_spread"), sem("head_turned")
        ones_ready, consts_landed = sem("ones_ready"), sem("consts_landed")
        conv_done, ln_summed = sem("conv_done"), sem("ln_summed")
        decay_ready, pads_ready, first_done = sem("decay_ready"), sem("pads_ready"), sem("first_done")
        rotated, centred = sem("rotated"), sem("centred")
        out_ready, out_stored = sem("out_ready"), sem("out_stored")

        block = ctx.enter_context(nc.Block())

        def split_jobs(one):
            def ahead(stage, g, turn=0):
                job = FIRST_JOB[stage] + g
                per = BODIES * TILES // JOB
                if isinstance(turn, int):
                    job, turn = job + per * turn, 0
                    if job + AHEAD > RUN_LAST[job]:
                        return
                one(job + AHEAD, turn)

            def start_run(stage):
                for i in range(AHEAD):
                    one(FIRST_JOB[stage] + i, 0)
            return ahead, start_run

        def raw_job(job):
            half, i = JOBS[job]
            return ring[:, half % SLOTS, i * JOB * P:(i + 1) * JOB * P]

        @block.sync
        def _(sp):
            sp.dma_start(x[:, :, 0:S], x_in[:, :, 0:S]).then_inc(x_landed, 16)

            def load(v, slot, tiles):
                src = wstream[v:v + 1, :, 0:tiles * P] if isinstance(v, int) else wstream[bass.ds(v, 1), :, 0:tiles * P]
                sp.dma_start(ring[:, slot, 0:tiles * P], src.rearrange("u p n -> (u p) n")).then_inc(landed[slot], 16)

            def free(v, turn):
                o = v - SLOTS
                if HALF_KIND[o] == SPLIT:
                    sp.wait_ge(weights_ready, turn * (SLOTS * HALF // JOB) + (LAST_JOB[o] + 1))
                elif HALF_KIND[o] == DIRECT:
                    sp.wait_ge(raw_used, turn * SLOTS + (PLACE[o] + 1))
                else:
                    sp.wait_ge(mod_summed, turn * SLOTS * DOTS + (PLACE[o] + 1) * DOTS)

            v = 0
            while v < HALVES:
                e = v
                while v >= SLOTS and e + SLOTS <= HALVES and all(
                        HALF_TILES[w] == HALF and HALF_TILES[w - SLOTS] == HALF and HALF_KIND[w - SLOTS] == HALF_KIND[v - SLOTS]
                        for w in range(e, e + SLOTS)):
                    e += SLOTS
                if e - v >= 2 * SLOTS:
                    with sp.Fori(0, (e - v) // SLOTS) as i:
                        for j in range(SLOTS):
                            free(v + j, i)
                            load(i * SLOTS + (v + j), (v + j) % SLOTS, HALF)
                    v = e
                    continue
                if v >= SLOTS:
                    free(v, 0)
                load(v, v % SLOTS, HALF_TILES[v])
                v += 1
                if v == 2:
                    sp.dma_start(prm[:], params_in).then_inc(params_landed, 16)
                    sp.dma_start(cst[:], consts_in).then_inc(consts_landed, 16)
                if v == SLOTS:
                    sp.dma_start(x[:, :, S:S2], x_in[:, :, S:S2]).then_inc(ctx_landed, 16)
            for slot in range(SLOTS):
                sp.wait_ge(landed[slot], 16 * len(range(slot, HALVES, SLOTS)))
            for k in range(KD):
                sp.wait_ge(out_ready, k + 1)
                sp.dma_start(out[:, k, :], f_out[:, k, :]).then_inc(out_stored, 16)
            sp.wait_ge(out_stored, 16 * KD)

        @block.gpsimd
        def _(pool):
            for e in range(2):
                nc.gpsimd.memset(mrow[:, e * S:(e + 1) * S], 0.0).then_inc(pool_written, 1)
            pstep = Count()

            def split_hidden(stage, units, products, hidden, N):
                for n, j, i in steps(pool, units, (pstep, 2)):
                    for e in range(2):
                        hi, lo = (v[:, bass.ds(n * 2 + e, 1), :].rearrange("p a b -> p (a b)")[:, 0:N] for v in hidden)
                        pool.wait_ge(acc_free[2 + e], n + (USED[stage][2 + e] + 1))
                        nc.gpsimd.tensor_copy(hi, products[:, e, 0:N]).then_inc(pool_step, 1)
                        pool.wait_ge(pool_step, pstep.next())
                        nc.gpsimd.tensor_tensor(lo, products[:, e, 0:N], hi.bitcast(F32), ALU.subtract).then_inc(pool_written, 1)

            pool.wait_ge(operand_ready, KL)
            for s in range(2):
                pool.dma_start(n_c[s], c_in[s]).then_inc(c_landed, 16)
            for l in range(2):
                split_hidden(f"ffn_in{l}", KF1 // 2, f_prod, f_hidden, S)
            for l in range(DEPTH):
                pool.wait_ge(rpb_place, l + 1)
                pool.dma_start(a_rpb.rearrange("p a b -> p (a b)"), rpb_in[l]).then_inc(rpb_landed, 16)
                pool.wait_ge(rpb_landed, 16 * (l + 1))
                pool.wait_ge(consts_landed, 16)
                nc.gpsimd.tensor_tensor(a_rpb, a_rpb, con("na_mask", 0, GRID).unsqueeze(1).broadcast_to([P, 48, GRID]),
                                        ALU.add).then_inc(rpb_ready, 1)
                if l == 0:
                    pool.wait_ge(o_free, (len(attention_jobs()) + len(attention_jobs(0))) // 4)
                    for s in range(2):
                        pool.dma_start(a_c[s], c_in[s]).then_inc(c_landed, 16)
                for p, units in (("a", HALF_A), ("b", HALF_B)):
                    split_hidden(f"mlp_in{l}{p}", units, m_prod, m_hidden, S2 if l == 0 else S)

        @block.tensor
        def _(pe):
            state = {"release": None, "closing": None}
            squares, hr, taken = Count(), Count(), Count()
            oper, aoper = Count(), Count()
            jobs_done = Count()

            def mm(*a, **k):
                ins = nc.tensor.matmul(*a, **k)
                if state["release"]:
                    ins.then_inc(state["release"], 1)
                state["release"], state["closing"] = state["closing"], None
                return ins

            def raw(stage, turn=0):
                def tile(t, n=1):
                    half = STAGE_HALVES[stage][t // HALF]
                    if t % HALF == 0:
                        pe.wait_ge(landed[half % SLOTS], turn * 16 + 16 * (half // SLOTS + 1))
                    if (t + n) % HALF == 0:
                        state["closing"] = raw_used
                    t %= HALF
                    return ring[:, half % SLOTS, t * P:(t + n) * P]
                return tile

            def job(stage, g, n=0):
                j = FIRST_JOB[stage] + g
                pe.wait_ge(weights_ready, n * 4 + (j + 1))

                def tile(t, count=1):
                    return [v[:, j % SPLITS, t * P:(t + count) * P] for v in (w_hi, w_lo)]
                return tile

            def job_done():
                assert state["release"] is None
                state["release"] = weights_used

            def product(o, left, right, start, stop):
                for i, (a, b) in enumerate(((0, 0), (0, 1), (1, 0))):
                    ins = mm(o, left[a], right[b], start=start and i == 0, stop=stop and i == 2)
                return ins

            def h_(k, a, b):
                return [v[:, k, a:b] for v in (h_hi, h_lo)]

            def free(stage, b, n):
                pe.wait_ge(acc_free[b], n + USED[stage][b])

            def norm(N):
                for k in range(KD):
                    pe.wait_ge(squares_ready, squares.next())
                    ins = nc.tensor.matmul(psO[:, 0:N], ones[:], sq[:, k % 4, 0:N], start=k == 0, stop=k == KD - 1)
                    if k:
                        ins.then_inc(sums_ready, 1)
                    elif state["release"]:
                        ins.then_inc(state["release"], 1)
                        state["release"] = None

            def gemm_group(banks, stage, u, n, N=S, first=0, between=None):
                for m in range(4):
                    w = job(stage, m, u)
                    free(banks, m, n)
                    for k in range(KD):
                        if first and m == 0:
                            pe.wait_ge(h_ready, hr.next(first))
                        ins = product(acc[m][:, 0:N], w(k), h_(k, 0, N), k == 0, k == KD - 1)
                    ins.then_inc(acc_full[m], 1)
                    job_done()
                    if between:
                        between(m)

            def turned_group(banks, first_bank, stage, tiles, width, wait=True):
                per = JOB * P // width if width > P else KD
                for k in range(KD):
                    if k % per == 0:
                        if k:
                            job_done()
                        w = job(stage[0], stage[1] + k // per)
                    for q in range(tiles):
                        if k == 0:
                            free(banks, first_bank + q, 0)
                        left, right = h_(k, q * P, (q + 1) * P), w(k % per * max(width // P, 1), max(width // P, 1))
                        ins = product(acc[first_bank + q][:, 0:width], left, [r[:, 0:width] for r in right], k == 0, k == KD - 1)
                        if k == KD - 1:
                            ins.then_inc(acc_full[first_bank + q], 1)
                job_done()

            def hidden_out(stage, chunks, src, N, ready):
                split = isinstance(src, list)
                w = None if split else raw(stage)
                for m in range(KD):
                    free(stage, m % 4, m // 4)
                    for k in range(chunks):
                        t = m * chunks + k
                        if m == 0:
                            ready(k)
                        if split:
                            if t % JOB == 0:
                                if t:
                                    job_done()
                                w = job(stage, t // JOB)
                            ins = product(acc[m % 4][:, 0:N], w(t % JOB), [v[:, k, 0:N] for v in src], k == 0, k == chunks - 1)
                        else:
                            ins = mm(acc[m % 4][:, 0:N], w(t), src[:, k, 0:N], start=k == 0, stop=k == chunks - 1)
                    ins.then_inc(acc_full[m % 4], 1)
                if split:
                    job_done()

            def modulation(l):
                stage = f"mod{l}"

                if l == 0:
                    pe.wait_ge(silu_ready, 1)
                assert state["release"]
                for n, j, i in steps(pe, 12 - MOD_V, (taken, 1)):
                    w = raw(stage, i)
                    free(stage, 3, n)
                    for k in range(KD):
                        ins = mm(acc[3][0:2, :], silc[:, k, :], w(j * TILES + 4 * k, 4), start=k == 0, stop=k == KD - 1)
                    ins.then_inc(acc_full[3], 1)
                    pe.wait_ge(acc_free[3], n + (USED[stage][3] + 1))
                    pe.wait_ge(mod_taken, taken.next())
                    for q in range(4):
                        ins = nc.tensor.transpose(psT[:, q * P:(q + 1) * P], mrow[:, q * P:(q + 1) * P], ident)
                    ins.then_inc(mod_turned, 1)

            def softmax(layer=None):
                jobs = attention_jobs(layer)
                base = jobs_done.base
                for j in range(len(jobs) + 5):
                    if j < len(jobs):
                        kind, t, p, q = jobs[j]
                        rows_ = slice(DH * p, DH * p + DH)
                        qs = slice(q * P, (q + 1) * P)
                        bank = score_banks[j % 3]
                        if j >= 3:
                            pe.wait_ge(prob_exp, base + j - 2)
                        if kind == "nsa":
                            nk = (q + 1) * P
                            ins = mm(bank[:].rearrange("p (b k) -> p b k", b=2)[:, :, 0:nk], n_q[rows_, t, qs],
                                     n_k[rows_, :, (2 * t + p) // GROUP, 0:nk], start=True, stop=True)
                        else:
                            a = 0 if q < 2 else S
                            key = a_nak[rows_, t, a:S2] if kind == "na" else a_gk[rows_, t // 2, a:S2]
                            qq = (a_naq if kind == "na" else a_gq)[rows_, t, qs]
                            ins = mm(bank[:, 0:S2 - a], qq, key, start=True, stop=True)
                        ins.then_inc(score_full, 1)
                    if 3 <= j < len(jobs) + 3:
                        i = j - 3
                        kind, t, p, q = jobs[i]
                        pe.wait_ge(prob_ready, base + i + 1)
                        if i >= 2:
                            pe.wait_ge(turned_ready, base + i - 1)
                        for b in turned_blocks(kind, q):
                            ins = nc.tensor.transpose(turn_banks[i % 2][:, b * P:(b + 1) * P], s_p[:, i % 4, b * P:(b + 1) * P], ident)
                        ins.then_inc(turned_full, 1)
                    if j >= 6 and j % 2 == 0:
                        i = j - 6
                        kind, t, p, q = jobs[i]
                        out_ = (base + i) // 4
                        o = out_banks[out_ % 2][DH * p:DH * p + DH, 0:S]
                        head = 2 * t + p
                        if p == 0 and out_ >= 2:
                            pe.wait_ge(o_free, out_ - 1)
                        pe.wait_ge(turned_ready, base + i + 2)
                        pT = (n_pT if kind == "nsa" else a_pT)[:, i % 4:i % 4 + 2, :]
                        terms = []
                        if kind == "nsa":
                            g = head // GROUP
                            terms.append((n_vz[:, head, :], n_pcT[:, :, g, :], 0))
                            for b in range(2):
                                for br in range(2):
                                    k = (br * 2 + b) * P
                                    terms.append((n_v[:, b, (br * KV + g) * DH:(br * KV + g + 1) * DH], pT[:, b:2, k:k + P], b))
                        else:
                            for n, b in enumerate(key_blocks(kind, q)):
                                v = a_nav[:, b, head * DH:(head + 1) * DH] if kind == "na" else a_gv[:, b, (t // 2) * DH:(t // 2 + 1) * DH]
                                terms.append((v, pT[:, :, n * P:(n + 1) * P], 0))
                        for n, (v, pr, first) in enumerate(terms):
                            ins = mm(o[:, first * P:], v, pr, start=n == 0, stop=n == len(terms) - 1)
                        ins.then_inc(o_full, 1)
                jobs_done.base += len(jobs)

            pe.wait_ge(ones_ready, 1)

            norm(S)
            for n in range(5):
                gemm_group("lru_in", "lru_in", n, n, first=int(n == 0))
            w = raw("lru_gate")
            for n in range(KL):
                b = n % 4
                free("lru_gate", b, n // 4)
                pe.wait_ge(acc_free[2 + n % 2], USED["lru_in"][2 + n % 2] + n // 2 + 1)
                mm(acc[b][:, 0:S], w(2 * n), l_x[:, n, :], start=True, stop=True)
                mm(acc[b][:, S:S2], w(2 * n + 1), l_x[:, n, :], start=True, stop=True).then_inc(acc_full[b], 1)
            state["release"] = raw_used
            pe.wait_ge(consts_landed, 16)
            modulation(0)
            hidden_out("lru_out", KL, l_y, S, lambda k: pe.wait_ge(operand_ready, oper.next()))

            def hidden_there(name, k):
                pe.wait_ge(pool_written, 2 + HIDDEN[name] + k + 1)

            def ffn(l):
                norm(S)
                for n, j, i in steps(pe, 12, peel=1):
                    gemm_group(f"ffn_in{l}", f"ffn_in{l}", n, n, first=int(isinstance(n, int) and n == 0))
                hidden_out(f"ffn_out{l}", KF1, f_hidden, S, lambda k: hidden_there(f"ffn{l}", k))

            ffn(0)

            norm(S)
            for n in range(2):
                gemm_group("nsa_q", "nsa_q", n, n, first=int(n == 0))
            for n in range(4):
                gemm_group("nsa_kv", "nsa_kv", n, n)
            turned_group("nsa_v", 0, ("nsa_v", 0), 2, 512)
            turned_group("nsa_gate", 2, ("nsa_gate", 0), 2, 48)
            w = raw("cmp")
            for kv in range(2):
                pe.wait_ge(operand_ready, oper.next())
                for m in range(2):
                    free("cmp", 2 * kv + m, 0)
                    for jj in range(HALF):
                        ins = mm(acc[2 * kv + m][:, 0:KV * NCMP], w((2 * kv + m) * HALF + jj), n_blk[:, kv * HALF + jj, :], start=jj == 0, stop=jj == HALF - 1)
                    ins.then_inc(acc_full[2 * kv + m], 1)
            for m in range(2):
                pe.wait_ge(acc_free[m], USED["cmp"][m] + 1)
            free("cmp2", 0, 0)
            for m in range(2):
                ins = mm(acc[0][:, 0:KV * NCMP], par("w2k", m * P, P), n_hid[:, m, :].rearrange("p (g c) -> p g c", c=CMPW)[:, :, 0:NCMP],
                         start=m == 0, stop=m == 1)
            ins.then_inc(acc_full[0], 1)
            pe.wait_ge(operand_ready, oper.next())
            free("cmp2", 1, 0)
            for g in range(KV):
                for m in range(2):
                    ins = mm(acc[1][:, g * DH:(g + 1) * DH], n_hv[:, m * KV + g, :], par("w2v", m * DH, DH), start=m == 0, stop=m == 1)
            ins.then_inc(acc_full[1], 1)
            pe.wait_ge(acc_free[0], USED["cmp2"][0] + 1)
            pe.wait_ge(acc_free[1], USED["cmp2"][1] + 1)
            for q in range(2):
                for head in range(HEADS):
                    t, p, g = head // 2, head % 2, head // GROUP
                    r_ = slice(DH * p, DH * p + DH)
                    ins = mm(cmp_banks[q][p][:, t * NCMP:(t + 1) * NCMP], n_q[r_, t, q * P:(q + 1) * P], n_ck[r_, 0, g * NCMP:(g + 1) * NCMP],
                             start=True, stop=True)
                ins.then_inc(pe_aux_full, 1)
            pe.wait_ge(operand_ready, oper.next(2))
            for q in range(2):
                for g in range(KV):
                    ins = nc.tensor.transpose((psT, psO)[q][:, g * P:(g + 1) * P], n_pc[:, q, g * P:(g + 1) * P], ident)
                ins.then_inc(pe_aux_full, 1)
            pe.wait_ge(pe_aux_free, 2)
            softmax()
            pe.wait_ge(o_free, jobs_done.base // 4)
            hidden_out("nsa_out", KD, n_q, S, lambda k: None)

            ffn(1)

            def dual(l):
                N = S2 if l == 0 else S
                norm(S2)
                for n in range(2):
                    gemm_group(f"conv_in{l}", f"in{l}", n, n, first=2 * int(n == 0), N=N)
                gemm_group(f"naq{l}", f"in{l}", 2, 0, N=N)
                gemm_group(f"nak{l}", f"in{l}", 3, 0, N=S2)
                turned_group(f"nav{l}", 0, (f"in{l}", 16), 4, 512)
                gemm_group(f"gq{l}", f"in{l}", 5, 0, N=N)
                for m in range(2):
                    w = job(f"in_gkv{l}", m)
                    free(f"gkv{l}", m, 0)
                    for k in range(KD):
                        ins = product(acc[m][:], w(k), h_(k, 0, S2), k == 0, k == KD - 1)
                    ins.then_inc(acc_full[m], 1)
                    job_done()
                w = job(f"in_gkv{l}", 2)
                for m in range(2):
                    free(f"gkv{l}", 2 + m, 0)
                    for e in range(2):
                        q = 2 * m + e
                        for k in range(KD):
                            ins = product(acc[2 + m][:, e * P:(e + 1) * P], h_(k, q * P, (q + 1) * P), w(k), k == 0, k == KD - 1)
                    ins.then_inc(acc_full[2 + m], 1)
                job_done()
                for i, c in enumerate((4, 5, 0, 1, 2, 3)):
                    n = N if c < 4 else S2
                    pe.wait_ge(act_operand_ready, aoper.next())
                    ins = mm(head_rows[0:12, 0:n], con("head_sel", 10 - 2 * c, 12), s_p[:, i % 4, 0:n], start=i == 0, stop=i == 5)
                    if i:
                        ins.then_inc(head_summed, 1)
                pe.wait_ge(operand_ready, oper.next())
                for c in range(8):
                    if c >= 2:
                        src = a_gq[:, c - 2, :] if c < 6 else a_gk[:, c - 6, :]
                        pe.wait_ge(operand_ready, oper.next())
                        if c >= 4:
                            pe.wait_ge(rotated, 6 * l + c - 3)
                        nc.tensor.matmul(head_turns[c % 2][:, 0:S], rope, src[:, 0:S], start=True, stop=True).then_inc(head_turned, 1)
                    if c < 6:
                        n = N if c < 4 else S2
                        for e in range(2):
                            row = ident[0:12, 2 * c + e:2 * c + e + 1].broadcast_to([12, DH])
                            ins = nc.tensor.matmul(head_factors[c % 2][e * DH:(e + 1) * DH, 0:n], row, rs[0:12, 0:n], start=True, stop=True)
                        ins.then_inc(head_spread, 1)
                pe.wait_ge(rotated, 6 * (l + 1))
                pe.wait_ge(acc_free[3], USED[f"gkv{l}"][3] + 1)
                pe.wait_ge(acc_free[1], USED[f"gkv{l}"][1] + 1)
                softmax(l)
                pe.wait_ge(o_free, jobs_done.base // 4)
                def conv_sums(n):
                    def between(m):
                        if (n, m) == (0, 3):
                            pe.wait_ge(conv_done, KC * (l + 1))
                            for c in range(KC):
                                ins = mm(psT[:, 0:N], ones[:], a_cy[:, c, 0:N], start=c == 0, stop=c == KC - 1)
                            ins.then_inc(pe_aux_full, 1)
                        if (n, m) == (1, 1):
                            for c in range(KC):
                                pe.wait_ge(act_operand_ready, aoper.next())
                                ins = mm(psO[:, 0:N], ones[:], s_p[:, c, 0:N], start=c == 0, stop=c == KC - 1)
                            ins.then_inc(ln_summed, 1)
                    return between

                for br in range(3):
                    src = (a_naq, a_gq, a_cy)[br]
                    for n in range(2):
                        gemm_group(f"gates{l}{br}", f"gates{l}{br}", n, n, N=N, between=conv_sums(n) if br == 0 else None)
                    w = raw(f"branch{l}{br}")
                    if br == 2:
                        pe.wait_ge(act_operand_ready, aoper.next(KC))
                    for m in range(KD):
                        free(f"branch{l}{br}", m % 4, m // 4)
                        for k in range(KC):
                            ins = mm(acc[m % 4][:, 0:N], w(m * KC + k), src[:, k, 0:N], start=k == 0, stop=k == KC - 1)
                        ins.then_inc(acc_full[m % 4], 1)
                hidden_out(f"out{l}", KD, [h_hi, h_lo], N, lambda k: pe.wait_ge(h_ready, hr.next()))
                norm(N)
                for p, units in (("a", HALF_A), ("b", HALF_B)):
                    for n, j, i in steps(pe, units, peel=int(p == "a")):
                        first = p == "a" and isinstance(n, int) and n == 0
                        gemm_group(f"mlp_in{l}{p}", f"mlp_in{l}{p}", n, n, N=N, first=N // S if first else 0)
                    hidden_out(f"mlp_out{l}{p}", 2 * units, m_hidden, N, lambda k: hidden_there(f"mlp{l}{p}", k))

            norm(S)
            for l in range(DEPTH):
                dual(l)
            norm(S)

        @block.scalar
        def _(act):
            tiles, scaled_c, jobs_done, sums = Count(), Count(), Count(), Count()
            cen = Count()

            def full(stage, b, n):
                act.wait_ge(acc_full[b], n + (USED[stage][b] + 1))

            def freed(stage, b, n):
                act.wait_ge(acc_free[b], n + (USED[stage][b] + 1))

            def go(o, i, f, **k):
                return nc.scalar.activation(o, i, f, **k)

            def root_of(N, bank, width, summed, rows=P):
                act.wait_ge(*summed)
                go(rs[0:rows, 0:N], bank[0:rows, 0:N], ACT.Sqrt, scale=1.0 / width, bias=eps[0:rows, :]).then_inc(root_ready, 1)

            def norm(N, ready, middle=None):
                for k in range(KD):
                    ready(k)
                    if k >= 4:
                        act.wait_ge(sums_ready, sums.base + max(k - 4, 1))
                    go(sq[:, k % 4, 0:N], x[:, k, 0:N], ACT.Square).then_inc(squares_ready, 1)
                sums.base += KD - 1
                if middle:
                    middle()
                root_of(N, psO, D, (sums_ready, sums.base))

            def h_norm(N, ready, bias=None, middle=None):
                norm(N, ready, middle)
                for k in range(KD):
                    for s in range(N // S):
                        n = k * (N // S) + s
                        act.wait_ge(scaled_ready, scaled_c.next())
                        o = h_hi[:, k, s * S:(s + 1) * S]
                        if bias is None:
                            ins = go(o, scaled[:, n % 8, :], ACT.Copy)
                        else:
                            ins = go(o, scaled[:, n % 8, :], ACT.Identity, bias=bias(k, s))
                        ins.then_inc(h_rounded, 1)

            def round_job(job, turn):
                half = JOBS[job][0]
                act.wait_ge(landed[half % SLOTS], turn * 16 + 16 * (half // SLOTS + 1))
                if job >= SPLITS:
                    act.wait_ge(weights_used, turn * (SLOTS * HALF // JOB) + (job - SPLITS + 1))
                go(w_hi[:, job % SPLITS, :], raw_job(job), ACT.Copy).then_inc(weights_rounded, 1)

            ahead, start_run = split_jobs(round_job)

            def after(stage):
                return lambda k: freed(stage, k % 4, k // 4)

            def copy(stage, b, n, o, i, func=ACT.Copy, **k):
                full(stage, b, n)
                go(o, i, func, **k).then_inc(acc_free[b], 1)

            def mod_row(l, n):
                copy(f"mod{l}", 3, n, mrow[0:2, :], acc[3][0:2, :])

            act.wait_ge(ones_ready, 1)
            act.wait_ge(x_landed, 16)
            h_norm(S, lambda k: None, middle=lambda: start_run("lru_in"))
            act.wait_ge(params_landed, 16)
            act.wait_ge(dve_tile_ready, tiles.next())
            go(sca[:, 0:10], sca[:, 0:10], ACT.Exp).then_inc(act_tile_ready, 1)
            go(silc.rearrange("p k s -> p (k s)"), par("c", 0, 2 * KD), ACT.Silu).then_inc(silu_ready, 1)
            for n in range(5):
                for j in range(4):
                    ahead("lru_in", 4 * n + j)
                    if j >= 2:
                        continue
                    copy("lru_in", j, n, l_y[:, 2 * n + j, :], acc[j][:, 0:S], func=ACT.Gelu_apprx_tanh)
            for n in range(KL):
                b = n % 4
                full("lru_gate", b, n // 4)
                go(l_r[:, n, :], acc[b][:, 0:S], ACT.Sigmoid, bias=par("gate_b", n))
                go(l_i[:, n, :], acc[b][:, S:S2], ACT.Sigmoid, bias=par("gate_b", KL + n)).then_inc(acc_free[b], 1)
            act.wait_ge(decay_ready, 1)
            act.wait_ge(pool_written, 2)
            freed("lru_gate", 1, 2)
            for n in range(KL):
                go(l_b[:, n, :], l_r[:, n, :], ACT.Exp, scale=sca[:, 20 + n:21 + n])
                go(l_t[:, n, :], l_r[:, n, :], ACT.Tanh, scale=sca[:, 30 + n:31 + n]).then_inc(act_tile_ready, 1)
                if n % 3 == 2:
                    mod_row(0, n // 3)
            for n in range(KL):
                act.wait_ge(dve_tile_ready, tiles.next())
                go(l_t[:, n, :], l_t[:, n, :], ACT.Sqrt, scale=2.0).then_inc(act_tile_ready, 1)
                if n < 9 - MOD_V:
                    mod_row(0, 3 + n)

            def ffn(l, before):
                start_run(f"ffn_in{l}")
                h_norm(S, after(before))
                st = f"ffn_in{l}"
                for n, j, i in steps(act, 12):
                    ahead(st, 4 * j, i)
                    for e in range(2):
                        ahead(st, 4 * j + 1 + e, i)
                        freed(st, e, n)
                        act.wait_ge(acc_free[2 + e], n + USED[st][2 + e])
                        go(f_gelu[:, e, :], f_conv[:, e, :], ACT.Gelu_apprx_tanh).then_inc(act_tile_ready, 1)
                    ahead(st, 4 * j + 3, i)
                for g in range(KD * KF1 // JOB):
                    ahead(f"ffn_out{l}", g)

            def softmax(layer=None):
                jobs = attention_jobs(layer)
                base = jobs_done.base
                for j in range(len(jobs) + 6):
                    if j < len(jobs):
                        kind, t, p, q = jobs[j]
                        act.wait_ge(score_max, base + j + 1)
                        if j >= 4:
                            act.wait_ge(turned_full, base + j - 3)
                        o, i = (used(v, kind, q) for v in (s_p[:, j % 4, :], score_banks[j % 3][:]))
                        for br in range(2 if kind == "nsa" else 1):
                            c = (j % 4) * 2 + br
                            ins = go(o[:, br, :], i[:, br, :], ACT.Exp, bias=s_max[:, c:c + 1], accum_out=s_sum[:, c:c + 1])
                        ins.then_inc(prob_exp, 1)
                    if 3 <= j < len(jobs) + 3:
                        n = j - 3
                        kind, t, p, q = jobs[n]
                        act.wait_ge(turned_full, base + n + 1)
                        if n >= 4:
                            act.wait_ge(o_full, base // 2 + (n - 4) // 2 + 1)
                        pT = n_pT if kind == "nsa" else a_pT
                        go(used(pT[:, n % 4, :], kind, q), used(turn_banks[n % 2][:], kind, q), ACT.Copy).then_inc(turned_ready, 1)
                    if j >= 9 and j % 4 == 1:
                        n = j - 9
                        kind, t, p, q = jobs[n]
                        out_ = (base + n) // 4
                        act.wait_ge(o_full, 2 * out_ + 2)
                        o = {"nsa": n_q, "na": a_naq, "gqa": a_gq}[kind]
                        go(o[:, t, q * P:(q + 2) * P], out_banks[out_ % 2][:, 0:S], ACT.Copy).then_inc(o_free, 1)
                jobs_done.base += len(jobs)

            ffn(0, "lru_out")
            act.wait_ge(c_landed, 32)
            for s in range(2):
                go(n_c[s], n_c[s], ACT.Silu).then_inc(c_ready, 1)
            h_norm(S, after("ffn_out0"))
            for n in range(2):
                for m in range(4):
                    ahead("nsa_q", 4 * n + m)
                    copy("nsa_q", m, n, n_q[:, 4 * n + m, :], acc[m][:, 0:S], scale=DH ** -0.5)
            for n in range(4):
                for m in range(4):
                    ahead("nsa_kv", 4 * n + m)
                    if n >= 2:
                        copy("nsa_kv", m, n, n_k[:, n - 2, m, :], acc[m][:, 0:S])
            for g in range(4):
                ahead("nsa_v", g)
            for q in range(2):
                copy("nsa_v", q, 0, n_v[:, q, :], acc[q][:])
            for q in range(2):
                copy("nsa_gate", 2 + q, 0, n_gate[:, q, :], acc[2 + q][:, 0:48], func=ACT.Sigmoid)
            act.wait_ge(pads_ready, 1)
            for i in range(4):
                copy("cmp", i, 0, n_hid[:, i, :].rearrange("p (g c) -> p g c", c=CMPW)[:, :, 0:NCMP],
                     acc[i][:, 0:KV * NCMP].rearrange("p (g c) -> p g c", c=NCMP), func=ACT.Gelu_apprx_tanh, bias=par("cmp_b1", i))
            for q in range(2):
                act.wait_ge(dve_tile_ready, tiles.next())
                go(s_p[:, q, 0:HEADS * NCMP], s_p[:, q, 0:HEADS * NCMP], ACT.Exp).then_inc(act_tile_ready, 1)
            softmax()
            ffn(1, "nsa_out")
            norm(S, after("ffn_out1"))

            def dual_norm(N, ready, l, shift):
                h_norm(N, ready, lambda k, s: mods[:, l, shift + k, s:s + 1])

            def dual(l):
                N = S2 if l == 0 else S
                if l == 0:
                    act.wait_ge(ctx_landed, 16)
                    dual_norm(S2, lambda k: act.wait_ge(first_done, k + 1), l, 0)
                else:
                    dual_norm(S2, after("mlp_out0b"), l, 0)
                for n in range(2):
                    for m in range(4):
                        ahead(f"in{l}", 4 * n + m)
                        if m >= 2:
                            e = m - 2
                            act.wait_ge(acc_free[e], USED[f"conv_in{l}"][e] + n)
                            copy(f"conv_in{l}", m, n, s_p[:, e, 0:N], acc[m][:, 0:N], func=ACT.Sigmoid)
                for m in range(4):
                    ahead(f"in{l}", 8 + m)
                    copy(f"naq{l}", m, 0, a_naq[:, m, 0:N], acc[m][:, 0:N], scale=DH ** -0.5)
                for m in range(4):
                    ahead(f"in{l}", 12 + m)
                    copy(f"nak{l}", m, 0, a_nak[:, m, :], acc[m][:])
                for m in range(4):
                    ahead(f"in{l}", 16 + m)
                for m in range(4):
                    copy(f"nav{l}", m, 0, a_nav[:, m, :], acc[m][:])
                for m in range(4):
                    ahead(f"in{l}", 20 + m)
                    copy(f"gq{l}", m, 0, a_gq[:, m, 0:N], acc[m][:, 0:N])
                for m in range(2):
                    ahead(f"in_gkv{l}", m)
                    copy(f"gkv{l}", m, 0, a_gk[:, m, :], acc[m][:])
                ahead(f"in_gkv{l}", 2)
                for m in range(2):
                    copy(f"gkv{l}", 2 + m, 0, a_gv[:, 2 * m:2 * m + 2, :].rearrange("p a b -> p (a b)"), acc[2 + m][:, 0:2 * P])
                freed(f"gkv{l}", 3, 0)
                act.wait_ge(conv_done, KC * (l + 1))
                for i, c in enumerate((4, 5, 0, 1, 2, 3)):
                    n = N if c < 4 else S2
                    src = a_gq[:, c, :] if c < 4 else a_gk[:, c - 4, :]
                    if i == 4:
                        act.wait_ge(head_summed, 5 * l + 1)
                    go(s_p[:, i % 4, 0:n], src[:, 0:n], ACT.Square).then_inc(act_operand_ready, 1)
                root_of(S2, head_rows, DH, (head_summed, 5 * (l + 1)), rows=12)
                softmax(l)
                for br in range(3):
                    for n in range(2):
                        for m in range(4):
                            ahead(f"gates{l}{br}", 4 * n + m)
                            copy(f"gates{l}{br}", m, n, a_sig[:, 4 * n + m, 0:N], acc[m][:, 0:N], func=ACT.Sigmoid)
                            if (l, br, n, m) == (0, 0, 0, 0):
                                act.wait_ge(c_landed, 64)
                                for s in range(2):
                                    go(a_c[s], a_c[s], ACT.Silu).then_inc(c_ready, 1)
                            if (br, n, m) == (0, 1, 0):
                                for c in range(KC):
                                    act.wait_ge(centred, cen.next())
                                    go(s_p[:, c, 0:N], a_cy[:, c, 0:N], ACT.Square).then_inc(act_operand_ready, 1)
                            if (br, n, m) == (0, 1, 1):
                                root_of(N, psO, CW, (ln_summed, l + 1))
                    if br == 0:
                        for c in range(KC):
                            act.wait_ge(centred, cen.next())
                            go(a_cy[:, c, 0:N], a_cy[:, c, 0:N], ACT.Silu, scale=par("ln_g", l * KC + c),
                               bias=par("ln_b", l * KC + c)).then_inc(act_operand_ready, 1)
                    start_run(f"gates{l}{br + 1}" if br < 2 else f"out{l}")
                for m in range(KD):
                    freed(f"branch{l}2", m % 4, m // 4)
                    go(h_hi[:, m, 0:N], a_y[:, m, 0:N], ACT.Copy).then_inc(h_rounded, 1)
                for g in range(KD * KD // JOB):
                    ahead(f"out{l}", g)
                dual_norm(N, after(f"out{l}"), l, 24)
                for p, units in (("a", HALF_A), ("b", HALF_B)):
                    st = f"mlp_in{l}{p}"
                    for n, j, i in steps(act, units):
                        for e in range(2):
                            ahead(st, 4 * j + e, i)
                            act.wait_ge(acc_free[2 + e], n + USED[st][2 + e])
                            copy(st, e, n, m_silu[:, e, 0:N], acc[e][:, 0:N], func=ACT.Silu)
                        for e in range(2):
                            ahead(st, 4 * j + 2 + e, i)
                    for g in range(2 * units):
                        ahead(f"mlp_out{l}{p}", g)

            for l in range(DEPTH):
                dual(l)
            norm(S, after("mlp_out1b"))

        @block.vector
        def _(dve):
            V = nc.vector
            step, roots, at, sums, aux, turn_c, jobs_done, rounded, hn = (Count() for _ in range(9))

            def link(ins):
                ins.then_inc(dve_step, 1)
                dve.wait_ge(dve_step, step.next())

            def full(stage, b, n):
                dve.wait_ge(acc_full[b], n + (USED[stage][b] + 1))

            def inverse(N):
                dve.wait_ge(root_ready, roots.next())
                link(V.reciprocal(rs[:, 0:N], rs[:, 0:N]))

            def norm(N, gain, to, signal):
                inverse(N)
                for k in range(KD):
                    V.scalar_tensor_tensor(out=to[:, k, 0:N], in0=x[:, k, 0:N], scalar=gain(k), in1=rs[:, 0:N],
                                           op0=ALU.mult, op1=ALU.mult).then_inc(signal, 1)

            def h_norm(N, gain, bias=None):
                inverse(N)
                tiles = [(k, s) for k in range(KD) for s in range(N // S)]
                for n in range(len(tiles) + 2):
                    if n < len(tiles):
                        k, s = tiles[n]
                        c = slice(s * S, (s + 1) * S)
                        if n >= 8:
                            dve.wait_ge(h_ready, hn.base + n - 7)
                        V.scalar_tensor_tensor(out=scaled[:, n % 8, :], in0=x[:, k, c], scalar=gain(k, s), in1=rs[:, c],
                                               op0=ALU.mult, op1=ALU.mult).then_inc(scaled_ready, 1)
                    if n >= 2:
                        k, s = tiles[n - 2]
                        c = slice(s * S, (s + 1) * S)
                        dve.wait_ge(h_rounded, rounded.next())
                        t, hi = scaled[:, (n - 2) % 8, :], h_hi[:, k, c].bitcast(F32)
                        if bias is None:
                            ins = V.tensor_tensor(h_lo[:, k, c], t, hi, ALU.subtract)
                        else:
                            ins = V.scalar_tensor_tensor(out=h_lo[:, k, c], in0=t, scalar=bias(k, s), in1=hi, op0=ALU.add, op1=ALU.subtract)
                        ins.then_inc(h_ready, 1)
                hn.base += len(tiles)

            def rest_job(job, turn):
                dve.wait_ge(weights_rounded, turn * (SLOTS * HALF // JOB) + (job + 1))
                V.tensor_tensor(w_lo[:, job % SPLITS, :], raw_job(job), w_hi[:, job % SPLITS, :].bitcast(F32),
                                ALU.subtract).then_inc(weights_ready, 1)

            ahead, start_run = split_jobs(rest_job)

            def out_jobs(stage, chunks, m):
                for g in range(-(-chunks * m // JOB), -(-chunks * (m + 1) // JOB)):
                    ahead(stage, g)

            def mod_take(l, n):
                if isinstance(n, int) and l + n == 0:
                    dve.wait_ge(mod_taken, 1)
                dve.wait_ge(mod_turned, turn_c.next())
                b = prm[:, bass.ds(n * 4 + (PARAM["b_mod"] + 48 * l), 4)]
                V.tensor_tensor(mods[:, l, bass.ds(n * 4, 4), :], psT[:].rearrange("p (a s) -> p a s", s=P)[:, :, 0:2],
                                b.unsqueeze(2).broadcast_to([P, 4, 2]), ALU.add).then_inc(mod_taken, 1)

            def mod_half(stage, i, c):
                v = STAGE_HALVES[stage][i]
                chunk = 2 * i + (48 - 4 * MOD_V if stage == "mod0v" else 0)
                dve.wait_ge(landed[v % SLOTS], 16 * (v // SLOTS + 1))
                for n in range(DOTS):
                    e, s, p = n // 4, n // 2 % 2, n % 2
                    if PLACE[v] + n // 2:
                        dve.wait_ge(mod_summed, PLACE[v] * DOTS + n - 1)
                    w = ring[:, v % SLOTS, (2 * e + p) * S2:(2 * e + p + 1) * S2]
                    V.scalar_tensor_tensor(out=ps[4 + p][:], in0=w, scalar=1.0, in1=c[s][:, p * S2:(p + 1) * S2], op0=ALU.mult,
                                           op1=ALU.mult, accum_out=mod_parts[:, chunk + e, s, p:p + 1]).then_inc(mod_summed, 1)

            def mod_finish(stage, l):
                halves = STAGE_HALVES[stage]
                a = 48 - 2 * len(halves)
                dve.wait_ge(mod_summed, DOTS * (PLACE[halves[-1]] + 1))
                m = mods[:, l, a:48, :]
                link(V.tensor_tensor(m, mod_parts[:, a:48, :, 0], mod_parts[:, a:48, :, 1], ALU.add))
                link(V.tensor_tensor(m, m, par("b_mod", 48 * l + a, 48 - a).unsqueeze(2).broadcast_to([P, 48 - a, 2]), ALU.add))

            def residual(stage, chunks=0, run=None):
                for m in range(KD):
                    out_jobs(stage, chunks, m)
                    full(stage, m % 4, m // 4)
                    V.tensor_tensor(x[:, m, 0:S], x[:, m, 0:S], acc[m % 4][:, 0:S], ALU.add).then_inc(acc_free[m % 4], 1)
                    if m == 3 and run:
                        start_run(run)

            V.memset(mods[:], 0.0).then_inc(mod_taken, 1)
            V.memset(eps[:], EPS)
            V.memset(ones[:], 1.0).then_inc(ones_ready, 1)
            start_run("lru_in")
            dve.wait_ge(params_landed, 16)
            dve.wait_ge(x_landed, 16)
            link(V.tensor_scalar(par("q_g", 0, 2), par("q_g", 0, 2), DH ** -0.5, None, ALU.mult))
            a_, e_, z_, z2_, s_ = par("a_param", 0, KL), sca[:, 0:10], sca[:, 10:20], sca[:, 20:30], sca[:, 30:40]
            link(V.tensor_scalar(e_, a_, -1.0, None, ALU.mult))
            V.tensor_tensor(e_, e_, a_, ALU.min).then_inc(dve_tile_ready, 1)
            h_norm(S, lambda k, s: par("lru_g", k))
            dve.wait_ge(act_tile_ready, at.next())
            link(V.tensor_scalar(z2_, e_, 2.0, None, ALU.add))
            link(V.reciprocal(z2_, z2_))
            link(V.tensor_tensor(z_, e_, z2_, ALU.mult))
            link(V.tensor_tensor(z2_, z_, z_, ALU.mult))
            link(V.tensor_scalar(s_, z2_, 1.0 / 15, 1.0 / 13, ALU.mult, ALU.add))
            for d in (11, 9, 7, 5, 3, 1):
                link(V.tensor_tensor(s_, s_, z2_, ALU.mult))
                link(V.tensor_scalar(s_, s_, 1.0 / d, None, ALU.add))
            link(V.tensor_tensor(s_, s_, z_, ALU.mult))
            link(V.tensor_scalar(e_, a_, -1.0, 0.0, ALU.mult, ALU.max))
            link(V.scalar_tensor_tensor(out=e_, in0=s_, scalar=2.0, in1=e_, op0=ALU.mult, op1=ALU.add))
            link(V.tensor_scalar(sca[:, 20:30], e_, -8.0, None, ALU.mult))
            V.tensor_scalar(sca[:, 30:40], e_, 8.0, None, ALU.mult).then_inc(decay_ready, 1)
            for n in range(5):
                ahead("lru_in", 4 * n)
                ahead("lru_in", 4 * n + 1)
                for e in range(2):
                    ahead("lru_in", 4 * n + 2 + e)
                    t = 2 * n + e
                    full("lru_in", 2 + e, n)
                    o, i = l_x[:, t, :], acc[2 + e][:, 0:S]
                    link(V.tensor_scalar(o, i, par("lru_cw", t * CONV_L + CONV_L - 1), par("lru_cb", t), ALU.mult, ALU.add))
                    for d in range(1, CONV_L):
                        ins = V.scalar_tensor_tensor(out=o[:, d:], in0=i[:, 0:S - d], scalar=par("lru_cw", t * CONV_L + CONV_L - 1 - d),
                                                     in1=o[:, d:], op0=ALU.mult, op1=ALU.add)
                        if d < CONV_L - 1:
                            link(ins)
                        else:
                            ins.then_inc(acc_free[2 + e], 1)
            for n in range(KL):
                dve.wait_ge(act_tile_ready, at.next())
                link(V.tensor_scalar(l_r[:, n, :], l_t[:, n, :], 1.0, None, ALU.add))
                link(V.reciprocal(l_r[:, n, :], l_r[:, n, :]))
                V.tensor_tensor(l_t[:, n, :], l_t[:, n, :], l_r[:, n, :], ALU.mult).then_inc(dve_tile_ready, 1)
                if n % 3 == 2:
                    mod_take(0, n // 3)
            for n in range(KL):
                dve.wait_ge(act_tile_ready, at.next())
                link(V.tensor_tensor(l_i[:, n, :], l_i[:, n, :], l_t[:, n, :], ALU.mult))
                link(V.tensor_tensor(l_i[:, n, :], l_i[:, n, :], l_x[:, n, :], ALU.mult))
                link(V.tensor_tensor_scan(l_r[:, n, :], l_b[:, n, :], l_i[:, n, :], 0.0, ALU.mult, ALU.add))
                V.tensor_tensor(l_y[:, n, :], l_y[:, n, :], l_r[:, n, :], ALU.mult).then_inc(operand_ready, 1)
                if n < 9 - MOD_V:
                    mod_take(0, 3 + n)
            residual("lru_out", run="ffn_in0")

            def product(name, n, e, o, gate, a):
                dve.wait_ge(pool_written, n * 2 + (HIDDEN[name] + e + 1))
                V.tensor_tensor(o, gate, a, ALU.mult).then_inc(acc_free[2 + e], 1)

            def ffn(l):
                h_norm(S, lambda k, s: par("ffn_g", l * KD + k))
                st = f"ffn_in{l}"

                def column(name, n, per, i):
                    return prm[:, bass.ds(n * per + (PARAM[name] + i), 1)]

                for n, j, i in steps(dve, 12, (step, 2 * CONV_F - 2), (at, 2)):
                    for e in range(2):
                        ahead(st, 4 * j + e, i)
                        full(st, e, n)
                        o, a = f_conv[:, e, :], acc[e][:, 0:S]
                        w = [column("ffn_cw", n, 2 * CONV_F, (l * KF1 + e) * CONV_F + d) for d in range(CONV_F)]
                        link(V.tensor_scalar(o, a, w[CONV_F - 1], column("ffn_cb", n, 2, l * KF1 + e), ALU.mult, ALU.add))
                        for d in range(1, CONV_F):
                            ins = V.scalar_tensor_tensor(out=o[:, d:], in0=a[:, 0:S - d], scalar=w[CONV_F - 1 - d], in1=o[:, d:],
                                                         op0=ALU.mult, op1=ALU.add)
                            if d < CONV_F - 1:
                                link(ins)
                            else:
                                ins.then_inc(acc_free[e], 1)
                    for e in range(2):
                        ahead(st, 4 * j + 2 + e, i)
                        full(st, 2 + e, n)
                        dve.wait_ge(act_tile_ready, at.next())
                        product(f"ffn{l}", n, e, f_prod[:, e, :], f_gelu[:, e, :], acc[2 + e][:, 0:S])
                residual(f"ffn_out{l}", KF1)

            def softmax(layer=None):
                jobs = attention_jobs(layer)
                base = jobs_done.base
                for j in range(len(jobs) + 1):
                    if j < len(jobs):
                        kind, t, p, q = jobs[j]
                        head = 2 * t + p
                        if kind == "na" and jobs[j - 1][0] != "na":
                            dve.wait_ge(rpb_ready, layer + 1)
                        dve.wait_ge(score_full, base + j + 1)
                        v = used(score_banks[j % 3][:], kind, q)
                        if kind == "nsa":
                            slope = float(np.float32(2.0 ** (-8.0 * (head + 1) / HEADS)))
                            nk = (q + 1) * P
                            c = con("causal", q * S, nk).unsqueeze(1).broadcast_to([P, 2, nk])
                            link(V.scalar_tensor_tensor(out=v, in0=c, scalar=slope, in1=v, op0=ALU.mult, op1=ALU.add))
                        if kind == "na" and q < 2:
                            bias = a_rpb[:, head * 6 + 2 - 2 * q:head * 6 + 6 - 2 * q, :].rearrange("p a b -> p (a b)")
                            sc = score_banks[j % 3][:, 0:S]
                            link(V.tensor_tensor(sc, sc, bias, ALU.add))
                        parts = 2 if kind == "nsa" else 1
                        i = (j % 4) * 2
                        V.tensor_reduce(s_max[:, i:i + parts], v, AX, ALU.max, negate=True).then_inc(score_max, 1)
                    if j >= 1:
                        kind, t, p, q = jobs[j - 1]
                        head = 2 * t + p
                        parts = 2 if kind == "nsa" else 1
                        i = ((j - 1) % 4) * 2
                        dve.wait_ge(prob_exp, base + j)
                        link(V.reciprocal(s_rec[:, i:i + parts], s_sum[:, i:i + parts]))
                        if kind == "nsa":
                            g = n_gate[:, q, HEADS + head:2 * HEADS + head + 1:HEADS]
                            link(V.tensor_tensor(s_rec[:, i:i + 2], s_rec[:, i:i + 2], g, ALU.mult))
                        o = used(s_p[:, (j - 1) % 4, :], kind, q)
                        for br in range(parts):
                            ins = V.tensor_scalar(o[:, br, :], o[:, br, :], s_rec[:, i + br:i + br + 1], None, ALU.mult)
                        ins.then_inc(prob_ready, 1)
                jobs_done.base += len(jobs)

            ffn(0)
            h_norm(S, lambda k, s: par("nsa_g", k))
            dve.wait_ge(consts_landed, 16)
            link(V.memset(n_hid, 0.0))
            link(V.memset(n_pc, 0.0))
            V.memset(n_vz, 0.0).then_inc(pads_ready, 1)
            for g in range(8):
                ahead("nsa_q", g)
            for n in range(2):
                for g in range(KV):
                    ahead("nsa_kv", 4 * n + g)
                    full("nsa_kv", g, n)
                    V.tensor_copy(n_kc[0:DH, n, g, :], acc[g][0:DH, 0:S])
                    V.tensor_copy(n_kc[DH:P, n, g, 0:S - 1], acc[g][DH:P, 1:S]).then_inc(acc_free[g], 1)
            for kv in range(2):
                dve.wait_ge(acc_free[3], USED["nsa_kv"][3] + kv + 1)
                for jj in range(HALF):
                    if jj % 4 == 0:
                        ahead("nsa_kv", 8 + 4 * kv + jj // 4)
                    o = n_blk[:, kv * HALF + jj, :].rearrange("p (g c) -> p g c", c=NCMP)
                    i = n_kc[:, kv, :, 2 * jj:2 * jj + CMP_STRIDE * (NCMP - 1) + 1:CMP_STRIDE]
                    ins = V.tensor_scalar(o, i, par("cmp_pos", kv * HALF + jj), None, ALU.add)
                ins.then_inc(operand_ready, 1)
                if kv == 1:
                    for g in range(4):
                        ahead("nsa_v", g)
            dve.wait_ge(c_ready, 2)
            for i in range(2 * MOD_V - 1):
                mod_half("mod0v", i, n_c)
            for m in range(2):
                dve.wait_ge(acc_free[2 + m], USED["cmp"][2 + m] + 1)
                for g in range(KV):
                    ins = V.tensor_copy(n_hv[:, m * KV + g, :].rearrange("p (r c) -> p r c", c=CMPW),
                                        n_hid[:, 2 + m, g * CMPW:(g + 1) * CMPW].unsqueeze(1).broadcast_to([P, 4, CMPW]))
            ins.then_inc(operand_ready, 1)
            mod_half("mod0v", 2 * MOD_V - 1, n_c)
            full("cmp2", 0, 0)
            V.tensor_copy(n_ck[:, 0, :], acc[0][:, 0:KV * NCMP]).then_inc(acc_free[0], 1)
            full("cmp2", 1, 0)
            dve.wait_ge(pads_ready, 1)
            vz = n_vz.rearrange("p (g r) d -> p g r d", r=GROUP)
            for r in range(GROUP):
                rows_ = slice(r * CMPW, (r + 1) * CMPW)
                ins = V.tensor_copy(vz[rows_, :, r, :], acc[1][rows_, 0:KV * DH].rearrange("p (g d) -> p g d", d=DH))
            ins.then_inc(acc_free[1], 1)
            mod_finish("mod0v", 0)
            W = HEADS * NCMP
            for q in range(2):
                sc = s_p[:, q, 0:W]
                sc3 = sc.rearrange("p (h c) -> p h c", c=NCMP)
                dve.wait_ge(pe_aux_full, aux.next())
                for p in range(2):
                    by_half = [v.rearrange("p (t e c) -> p t e c", e=2, c=NCMP)[:, :, p, :] for v in (sc, con("cmp_bias", q * W, W))]
                    ins = V.tensor_tensor(by_half[0], cmp_banks[q][p][:, 0:W // 2].rearrange("p (t c) -> p t c", c=NCMP), by_half[1], ALU.add)
                link(ins)
                link(V.tensor_reduce(s_cm, sc3, AX, ALU.max))
                V.tensor_tensor(sc3, sc3, s_cm.unsqueeze(2).broadcast_to([P, HEADS, NCMP]), ALU.subtract).then_inc(dve_tile_ready, 1)
                dve.wait_ge(act_tile_ready, at.next())
                link(V.reduce_sum(s_cs, sc3, AX))
                link(V.reciprocal(s_cr, s_cs))
                link(V.tensor_tensor(s_cr, s_cr, n_gate[:, q, 0:HEADS], ALU.mult))
                link(V.tensor_tensor(sc3, sc3, s_cr.unsqueeze(2).broadcast_to([P, HEADS, NCMP]), ALU.mult))
                V.tensor_tensor(n_pc[:, q, :].rearrange("p (h c) -> p h c", c=CMPW)[:, :, 0:NCMP], sc3,
                                con("cmp_mask", q * NCMP, NCMP).unsqueeze(1).broadcast_to([P, HEADS, NCMP]), ALU.mult).then_inc(operand_ready, 1)
                dve.wait_ge(operand_ready, KL + 3 + q + 1)
            for q in range(2):
                dve.wait_ge(pe_aux_full, aux.next())
                V.tensor_copy(n_pcT[:, q, :, :].rearrange("p g k -> p (g k)"), (psT, psO)[q][:]).then_inc(pe_aux_free, 1)
            softmax()
            residual("nsa_out", run="ffn_in1")
            ffn(1)
            norm(S, lambda k: par("final_g", k), x, first_done)

            def dual_residual(stage, l, gate, N, chunks):
                for m in range(KD):
                    out_jobs(stage, chunks, m)
                    full(stage, m % 4, m // 4)
                    for s in range(N // S):
                        o = x[:, m, s * S:(s + 1) * S]
                        ins = V.scalar_tensor_tensor(out=o, in0=acc[m % 4][:, s * S:(s + 1) * S], scalar=mods[:, l, gate + m, s:s + 1], in1=o,
                                                     op0=ALU.mult, op1=ALU.add)
                    ins.then_inc(acc_free[m % 4], 1)

            def dual_norm(N, which, l):
                h_norm(N, lambda k, s: gn[:, which, s, k:k + 1], lambda k, s: mods[:, l, 24 * which + k, s:s + 1])

            def dual(l):
                N = S2 if l == 0 else S
                ns = N // S
                for which in range(2):
                    for s in range(2):
                        link(V.scalar_tensor_tensor(out=gn[:, which, s, :], in0=mods[:, l, 24 * which + 8:24 * which + 16, s], scalar=1.0,
                                                    in1=par(f"norm{which + 1}", l * KD, KD), op0=ALU.add, op1=ALU.mult))
                dual_norm(S2, 0, l)
                link(V.memset(a_u[:, :, 0:HALO], 0.0))
                V.memset(a_u[:, :, HALO + S:], 0.0).then_inc(rpb_place, 1)
                for n in range(2):
                    ahead(f"in{l}", 4 * n)
                    ahead(f"in{l}", 4 * n + 1)
                    for e in range(2):
                        ahead(f"in{l}", 4 * n + 2 + e)
                        full(f"conv_in{l}", e, n)
                        dve.wait_ge(acc_free[2 + e], USED[f"conv_in{l}"][2 + e] + n + 1)
                        V.tensor_tensor(a_u3[:, 2 * n + e, 0:ns, HALO:HALO + S], acc[e][:, 0:N].rearrange("p (s t) -> p s t", t=S),
                                        s_p[:, e, 0:N].rearrange("p (s t) -> p s t", t=S), ALU.mult).then_inc(acc_free[e], 1)
                for e in range(2):
                    dve.wait_ge(acc_free[e], USED[f"conv_in{l}"][e] + 2)
                cy = a_cy.rearrange("p c (s t) -> p c s t", t=S)

                def conv(c, j):
                    w = prm[:, bass.ds(j + (PARAM["conv_w"] + (l * KC + c) * CONV_K), 1)]
                    return V.scalar_tensor_tensor(out=cy[:, c, 0:ns, :], in0=a_u3[:, c, 0:ns, bass.ds(j, S)], scalar=w, in1=cy[:, c, 0:ns, :],
                                                  op0=ALU.mult, op1=ALU.add)

                for c in range(KC):
                    V.tensor_scalar(cy[:, c, 0:ns, :], a_u3[:, c, 0:ns, 0:S], par("conv_w", (l * KC + c) * CONV_K), par("conv_b", l * KC + c),
                                    ALU.mult, ALU.add).then_inc(dve_step, 1)
                def tap(j):
                    for c in range(KC):
                        dve.wait_ge(dve_step, j * KC + (step.base + c - KC + 1))
                        conv(c, j).then_inc(dve_step, 1)

                per_job = [2, 2, 2, 2, 2, 2, 1, 1]
                with dve.Fori(0, 2) as i:
                    for g in range(8):
                        ahead(f"in{l}", 8 + g, i)
                        for t in range(per_job[g]):
                            tap(i * sum(per_job) + (sum(per_job[:g]) + t + 1))
                tap(CONV_K - 2)
                step.base += (CONV_K - 1) * KC
                dve.wait_ge(dve_step, step.base)
                for c in range(KC):
                    conv(c, CONV_K - 1).then_inc(conv_done, 1)
                for g in range(3):
                    ahead(f"in_gkv{l}", g)
                dve.wait_ge(conv_done, KC * (l + 1))
                dve.wait_ge(root_ready, roots.next())
                V.reciprocal(rs[0:12, :], rs[0:12, :]).then_inc(operand_ready, 1)
                for c in range(7):
                    if c < 6:
                        n = N if c < 4 else S2
                        src = (a_gq[:, c, :] if c < 4 else a_gk[:, c - 4, :])[:, 0:n]
                        dve.wait_ge(head_spread, 6 * l + c + 1)
                        V.scalar_tensor_tensor(out=src, in0=src, scalar=par("q_g" if c < 4 else "k_g", l), in1=head_factors[c % 2][:, 0:n],
                                               op0=ALU.mult, op1=ALU.mult).then_inc(operand_ready, 1)
                    if c:
                        src = (a_gq[:, c - 1, :] if c < 5 else a_gk[:, c - 5, :])[:, 0:S]
                        dve.wait_ge(head_turned, 6 * l + c)
                        V.tensor_tensor(s_p[:, 3, 0:S], head_turns[(c - 1) % 2][:, 0:S], con("sin", 0, S), ALU.mult).then_inc(dve_step, 1)
                        link(V.tensor_tensor(src, src, con("cos", 0, S), ALU.mult))
                        dve.wait_ge(dve_step, step.next())
                        V.tensor_tensor(src, src, s_p[:, 3, 0:S], ALU.add).then_inc(rotated, 1)
                        dve.wait_ge(rotated, 6 * l + c)
                softmax(l)
                for br in range(3):
                    st = f"branch{l}{br}"
                    for g in range(8):
                        ahead(f"gates{l}{br}", g)
                        if (br, g) == (0, 4):
                            dve.wait_ge(pe_aux_full, aux.next())
                            link(V.tensor_scalar(rs[:, 0:N], psT[:, 0:N], 1.0 / CW, None, ALU.mult))
                            for c in range(KC):
                                V.tensor_tensor(a_cy[:, c, 0:N], a_cy[:, c, 0:N], rs[:, 0:N], ALU.subtract).then_inc(centred, 1)
                        if (br, g) == (0, 5):
                            inverse(N)
                            for c in range(KC):
                                V.tensor_tensor(a_cy[:, c, 0:N], a_cy[:, c, 0:N], rs[:, 0:N], ALU.mult).then_inc(centred, 1)
                        if l == 0 and g >= 1:
                            if (br, g) == (0, 1):
                                                                dve.wait_ge(c_ready, 4)
                            mod_half("mod1", 8 * br + g - 1, a_c)
                    for m in range(KD + 2 * (br == 2)):
                        if m == 2:
                            if l == 0:
                                mod_half("mod1", 8 * br + 7, a_c)
                            start_run(f"gates{l}{br + 1}" if br < 2 else f"out{l}")
                        if br == 2 and m >= 2:
                            dve.wait_ge(h_rounded, rounded.next())
                            V.tensor_tensor(h_lo[:, m - 2, 0:N], a_y[:, m - 2, 0:N], h_hi[:, m - 2, 0:N].bitcast(F32), ALU.subtract).then_inc(h_ready, 1)
                        if m >= KD:
                            continue
                        full(st, m % 4, m // 4)
                        if m < 4:
                            dve.wait_ge(acc_free[m], USED[f"gates{l}{br}"][m] + 2)
                        o, g, a = a_y[:, m, 0:N], a_sig[:, m, 0:N], acc[m % 4][:, 0:N]
                        if br == 0:
                            V.tensor_tensor(o, a, g, ALU.mult).then_inc(acc_free[m % 4], 1)
                        else:
                            link(V.tensor_tensor(s_p[:, m % 2, 0:N], a, g, ALU.mult))
                            V.tensor_tensor(o, o, s_p[:, m % 2, 0:N], ALU.add).then_inc(acc_free[m % 4], 1)
                if l == 0:
                    mod_finish("mod1", 1)
                hn.base += KD
                dual_residual(f"out{l}", l, 16, N, KD)
                dual_norm(N, 1, l)
                for p, units in (("a", HALF_A), ("b", HALF_B)):
                    st = f"mlp_in{l}{p}"
                    for n, j, i in steps(dve, units):
                        ahead(st, 4 * j, i)
                        ahead(st, 4 * j + 1, i)
                        for e in range(2):
                            ahead(st, 4 * j + 2 + e, i)
                            full(st, 2 + e, n)
                            dve.wait_ge(acc_free[e], n + (USED[st][e] + 1))
                            product(f"mlp{l}{p}", n, e, m_prod[:, e, 0:N], m_silu[:, e, 0:N], acc[2 + e][:, 0:N])
                    dual_residual(f"mlp_out{l}{p}", l, 40, N, 2 * units)

            for l in range(DEPTH):
                dual(l)
            norm(S, lambda k: par("final2", k), f_out, out_ready)


def constants():
    c = np.zeros((P, CONST["end"]), np.float32)

    def put(name, a):
        a = a.reshape(P, -1)
        c[:, CONST[name]:CONST[name] + a.shape[1]] = a

    put("ident", np.eye(P))
    p = np.arange(P)
    put("head_sel", (p[:, None] // DH == np.arange(22)[None, :] - 10).astype(np.float32))
    r = np.zeros((P, P))
    for i in range(P):
        if i % 32 < 16:
            r[i + 16, i] = -1.0
        else:
            r[i - 16, i] = 1.0
    put("rope", r)
    half = DH // 2
    freqs = np.power(np.float32(10000.0), -np.arange(0, half, 2, dtype=np.float32) / half).astype(np.float32)
    t = np.arange(S)
    ang = np.zeros((P, S), np.float32)
    for i in range(P):
        ang[i] = (t // GRID if i % DH < half else t % GRID).astype(np.float32) * freqs[i % 16]
    put("cos", np.cos(ang))
    put("sin", np.sin(ang))
    q = np.arange(S).reshape(2, P)
    dist = q[:, :, None] - np.arange(S)[None, None, :]
    put("causal", np.where(dist >= 0, -dist, NEG).transpose(1, 0, 2))
    start = np.arange(NCMP) * CMP_STRIDE
    end, centre = start + CMP_BLOCK - 1, start + (CMP_BLOCK - 1) / 2.0
    slopes = (2.0 ** (-8.0 * np.arange(1, HEADS + 1) / HEADS)).astype(np.float32)
    ok = end[None, None, :] <= q[:, :, None]
    d = (q[:, :, None] - centre[None, None, :]).astype(np.float32)
    b = np.where(ok[:, :, None, :], -slopes[None, None, :, None] * d[:, :, None, :], NEG)
    put("cmp_bias", b.transpose(1, 0, 2, 3))
    put("cmp_mask", ok.astype(np.float32).transpose(1, 0, 2))
    win0 = np.clip(p % GRID - 8, 0, GRID - 16)[:, None]
    kc = np.arange(GRID)[None, :]
    put("na_mask", np.where((kc >= win0) & (kc < win0 + 16), 0.0, NEG))
    return c


def tiles_of(w):
    k, m = w.shape
    return w.reshape(k // P, P, m // P, P).transpose(2, 0, 1, 3).reshape(-1, P, P)


def rows_of(w):
    k, m = w.shape
    return w.reshape(k // P, P, m // P, P).transpose(0, 2, 1, 3).reshape(-1, P, P)


def twice(w):
    k, m = w.shape
    w = w.reshape(k, m // DH, 1, DH)
    return np.concatenate([w, w], axis=2).reshape(k, 2 * m)


def pairs(w, half, width=2 * P):
    return [tiles_of(np.concatenate([w[:, i:i + width], w[:, half + i:half + i + width]], axis=1)) for i in range(0, half, width)]


def weight_stream(a):
    out = np.zeros((HALVES, P, HALF, P), np.float32)
    tiles = {name: sum(s[1] for s in STREAM if s[0] == name) for name in STAGE_HALVES}

    def put(name, *parts):
        t = 0
        for part in parts:
            for tile in part:
                out[STAGE_HALVES[name][t // HALF], :, t % HALF, :] = tile
                t += 1
        assert tiles[name] == t, (name, t)

    put("lru_in", *pairs(a["lru_w_in"][0], LRU))
    put("lru_gate", a["lru_gate_w"][0].transpose(1, 0, 2, 3).reshape(2 * KL, P, P))
    put("lru_out", tiles_of(a["lru_w_out"][0]))
    first = 12 - MOD_V
    put("mod0", *[rows_of(a["w_mod_2"][0][:, i:i + 512]) for i in range(0, first * 512, 512)])
    put("mod0v", a["w_mod_2"][0].reshape(KD, P, 48, P).transpose(2, 0, 3, 1)[4 * first:].reshape(-1, P, P))
    put("mod1", a["w_mod_2"][1].reshape(KD, P, 48, P).transpose(2, 0, 3, 1).reshape(-1, P, P))
    for l in range(DEPTH):
        put(f"ffn_in{l}", *pairs(a["ffn_w_in"][l], FF1))
        put(f"ffn_out{l}", tiles_of(a["ffn_w_out"][l]))
    w = a["nsa_w_in"][0]
    put("nsa_q", tiles_of(w[:, 0:D]))
    kv = w[:, D:D + 1536].reshape(D, 3, 2, KV * DH)
    put("nsa_kv", *[tiles_of(twice(kv[:, b, c])) for b, c in ((0, 0), (0, 1), (1, 0), (2, 0))])
    put("nsa_v", rows_of(np.concatenate([kv[:, 1, 1], kv[:, 2, 1]], axis=1)))
    g = np.zeros((D, P), np.float32)
    g[:, 0:48] = w[:, D + 1536:]
    put("nsa_gate", rows_of(g))
    put("cmp", *[tiles_of(a["nsa_cmp_w1"][0, i]) for i in range(2)])
    put("nsa_out", tiles_of(a["nsa_w_out"][0]))
    for l in range(DEPTH):
        w = a["w_in_2"][l]
        o = np.cumsum([0, 1024, 512, 512, 512, 512, 128, 128, 3072])
        put(f"in{l}", *pairs(w[:, 0:1024], 512), tiles_of(w[:, o[1]:o[2]]), tiles_of(w[:, o[2]:o[3]]), rows_of(w[:, o[3]:o[4]]),
            tiles_of(w[:, o[4]:o[5]]))
        put(f"in_gkv{l}", tiles_of(twice(w[:, o[5]:o[6]])), rows_of(w[:, o[6]:o[7]]))
        for b, (name, at) in enumerate((("w_na_out_2", 1), ("w_gqa_out_2", 2), ("w_conv_out_2", 0))):
            put(f"gates{l}{b}", tiles_of(w[:, o[7] + at * D:o[7] + (at + 1) * D]))
            put(f"branch{l}{b}", tiles_of(a[name][l]))
        put(f"out{l}", tiles_of(a["w_out_2"][l]))
        w = pairs(a["w_ffn_in_2"][l], FF2)
        put(f"mlp_in{l}a", *w[:HALF_A])
        put(f"mlp_in{l}b", *w[HALF_A:])
        put(f"mlp_out{l}a", tiles_of(a["w_ffn_out_2"][l][:HALF_A * 2 * P]))
        put(f"mlp_out{l}b", tiles_of(a["w_ffn_out_2"][l][HALF_A * 2 * P:]))
    return out.reshape(HALVES, P, HALF * P)


def parameters(a):
    out = np.zeros((P, PARAM["end"]), np.float32)

    def put(name, v):
        v = v.reshape(P, -1)
        out[:, PARAM[name]:PARAM[name] + v.shape[1]] = v

    def col(v):
        n = v.shape[-1] // P
        return np.moveaxis(v.reshape(v.shape[:-1] + (n, P)), -1, 0)

    def taps(w):
        l, k, c = w.shape
        return w.reshape(l, k, c // P, P).transpose(3, 0, 2, 1)

    for name, key in (("lru_g", "lru_norm_g"), ("nsa_g", "nsa_norm_g"), ("ffn_g", "ffn_norm_g"), ("final_g", "final_norm_g"),
                      ("norm1", "norm1_g_2"), ("norm2", "norm2_g_2"), ("final2", "final_g_2"), ("lru_cb", "lru_conv_b"),
                      ("gate_b", "lru_gate_b"), ("a_param", "lru_a_param"), ("ffn_cb", "ffn_conv_b"), ("cmp_b1", "nsa_cmp_b1"),
                      ("b_mod", "b_mod_2"), ("conv_b", "conv_b_2"), ("ln_g", "conv_ln_g_2"), ("ln_b", "conv_ln_b_2")):
        put(name, col(a[key]))
    for name, key in (("lru_cw", "lru_conv_w"), ("ffn_cw", "ffn_conv_w"), ("conv_w", "conv_w_2")):
        put(name, taps(a[key]))
    put("cmp_pos", a["nsa_cmp_pos"][0].reshape(2, HALF, P).transpose(2, 0, 1))
    for name, key in (("q_g", "q_norm_g_2"), ("k_g", "k_norm_g_2")):
        put(name, np.concatenate([a[key].T, a[key].T], axis=0))
    put("c", np.stack([a["c_2"][0].reshape(KD, P).T, a["c_ctx_2"].reshape(KD, P).T], axis=2))
    w2 = a["nsa_cmp_w2"][0].reshape(2, 2, P, DH)
    put("w2k", np.concatenate([w2[0], w2[0]], axis=2).transpose(1, 0, 2))
    put("w2v", w2[1].transpose(1, 0, 2))
    return out


def position_biases(rpb):
    r, qc = np.arange(P) // GRID, np.arange(P) % GRID
    rows = 4 + np.arange(6)[None, :] + (1 - r)[:, None]
    cols = np.clip(np.arange(GRID)[None, :] - qc[:, None] + 15, 0, 30)
    b = rpb[:, :, rows[:, :, None], cols[:, None, :]]
    return np.ascontiguousarray(b.transpose(0, 2, 1, 3, 4)).reshape(rpb.shape[0], P, -1)


def layout(inputs):
    a = {k: np.asarray(v) for k, v in inputs.items()}
    both = np.concatenate([a["x"][0].T.reshape(KD, P, S), a["ctx_2"][0].T.reshape(KD, P, S)], axis=2)
    return {"wstream": weight_stream(a), "params": parameters(a), "consts": constants(),
            "rpb": position_biases(a["na_rpb_2"]),
            "c_in": np.ascontiguousarray(np.broadcast_to(np.stack([a["c_2"][0], a["c_ctx_2"]]).reshape(2, 1, D), (2, P, D))), "x_in": np.ascontiguousarray(both.transpose(1, 0, 2))}


SHAPES = {"wstream": (HALVES, P, HALF * P), "params": (P, PARAM["end"]), "consts": (P, CONST["end"]),
          "rpb": (DEPTH, P, 48 * GRID), "c_in": (2, P, D), "x_in": (P, KD, S2)}


def kernel(**inputs):
    import concourse.bacc as bacc
    from concourse.bass_utils import run_bass_kernel_spmd

    nc = bacc.Bacc("TRN2", target_bir_lowering=False, num_devices=1)
    aps = [nc.dram_tensor(n, s, F32, kind="ExternalInput").ap() for n, s in SHAPES.items()]
    out = nc.dram_tensor("out", (P, KD, S), F32, kind="ExternalOutput").ap()
    program(nc, *aps, out)
    r = run_bass_kernel_spmd(nc, [layout(inputs)], core_ids=[0])
    out = r.results[0]["out"]
    return np.ascontiguousarray(out.transpose(2, 1, 0)).reshape(1, S, D)
```
